# Optimizing a Trainium2 kernel written in Bass

```python
import jax, jax.numpy as jnp
from jax import lax
import numpy as np

D_MODEL = 2048
BATCH = 1
SEQ = 256
DEPTH = 1

CTX_LEN = 256
GRID_W = 64
N_BRANCH = 4
BRANCH_W = D_MODEL // N_BRANCH
GROUP_W = 128
N_GROUPS = BRANCH_W // GROUP_W
N_IN_SLICES = 8
IN_W = N_IN_SLICES * BRANCH_W
POOL_WINDOWS = (2, 4, 8, 16)
CHUNK = 128
CONV_W = 4
LRU_C = 8.0
NA_HEADS = N_GROUPS
NA_HEAD_DIM = GROUP_W
NA_WIN_R = 8
NA_WIN_C = 16
D_FF = -(-(8 * D_MODEL) // (3 * 256)) * 256
EPS = 1e-6
NEG_INF = -1e30

kernel_name = "hybrid_pool_sgu_rglru_natten_gated_merge"

def rms_norm(x, g):
    xf = x.astype(jnp.float32)
    y = xf * lax.rsqrt(jnp.mean(xf * xf, axis=-1, keepdims=True) + EPS)
    return (y * g.astype(jnp.float32)).astype(x.dtype)

def layer_norm(x, g):
    xf = x.astype(jnp.float32)
    xc = xf - jnp.mean(xf, axis=-1, keepdims=True)
    y = xc * lax.rsqrt(jnp.mean(xc * xc, axis=-1, keepdims=True) + EPS)
    return (y * g.astype(jnp.float32)).astype(x.dtype)

def adaln(cond, w_mod, b_mod):
    m = (jax.nn.silu(cond) @ w_mod + b_mod).reshape(cond.shape[:-1] + (6, D_MODEL))
    return tuple(jnp.expand_dims(m[..., i, :], -2) for i in range(6))

def modulate(xn, shift, scale):
    return xn * (1.0 + scale) + shift

def heads(z):
    return z.reshape(z.shape[0], z.shape[1], NA_HEADS, NA_HEAD_DIM)

def block_diag_linear(z, w, b):
    B, L, _ = z.shape
    y = jnp.einsum('blgc,gcd->blgd', z.reshape(B, L, N_GROUPS, GROUP_W), w)
    return y.reshape(B, L, BRANCH_W) + b

def pool_branch(z, w_pool, pool_scale):
    B, L, _ = z.shape
    zf = z.astype(jnp.float32)
    cs = jnp.concatenate([jnp.zeros((B, 1, BRANCH_W), jnp.float32), jnp.cumsum(zf, axis=1)], axis=1)
    t = jnp.arange(L)
    outs = []
    for gi, w in enumerate(POOL_WINDOWS):
        lo = jnp.clip(t - w // 2, 0, L)
        hi = jnp.clip(t + w // 2, 0, L)
        sl = slice(gi * GROUP_W, (gi + 1) * GROUP_W)
        csg = cs[..., sl]
        mean = (csg[:, hi] - csg[:, lo]) / (hi - lo).astype(jnp.float32)[None, :, None]
        outs.append(mean - zf[..., sl])
    pooled = jnp.concatenate(outs, axis=-1).astype(z.dtype)
    y = jnp.einsum('blgc,gcd->blgd', pooled.reshape(B, L, N_GROUPS, GROUP_W), w_pool)
    return y.reshape(B, L, BRANCH_W) * pool_scale

def spatial_gating(u, v, ln_g, w_sp, b_sp):
    B, L, _ = v.shape
    vn = layer_norm(v, ln_g).reshape(B, L // CHUNK, CHUNK, N_GROUPS, GROUP_W)
    mixed = jnp.einsum('gpq,bnqgc->bnpgc', w_sp, vn) + b_sp.T[None, None, :, :, None]
    return u * mixed.reshape(B, L, BRANCH_W)

def centred_depthwise_conv(z, w, b):
    L = z.shape[1]
    left = CONV_W // 2
    zp = jnp.pad(z, ((0, 0), (left, CONV_W - 1 - left), (0, 0)))
    out = zp[:, 0:L] * w[0] + b
    for k in range(1, CONV_W):
        out = out + zp[:, k:k + L] * w[k]
    return out

def _affine_combine(lhs, rhs):
    a_l, b_l = lhs
    a_r, b_r = rhs
    return a_l * a_r, a_r * b_l + b_r

def rg_lru(z, w_r, b_r, w_i, b_i, lam, h0, reverse):
    r = jax.nn.sigmoid(block_diag_linear(z, w_r, b_r).astype(jnp.float32))
    i = jax.nn.sigmoid(block_diag_linear(z, w_i, b_i).astype(jnp.float32))
    log_a = -LRU_C * r * jax.nn.softplus(-lam.astype(jnp.float32))
    a = jnp.exp(log_a)
    b = jnp.sqrt(-jnp.expm1(2.0 * log_a)) * (i * z.astype(jnp.float32))
    a_cum, b_cum = lax.associative_scan(_affine_combine, (a, b), axis=1, reverse=reverse)
    return a_cum * h0[:, None, :] + b_cum

def neighbourhood_attention(q, k, v, k_ctx, v_ctx, rpb):
    B, L, H, Dh = q.shape
    rows = L // GRID_W
    wr = min(NA_WIN_R, rows)
    r_idx = jnp.arange(rows)
    key_rows = jnp.clip(r_idx - wr // 2, 0, rows - wr)[:, None] + jnp.arange(wr)[None, :]
    col = jnp.arange(GRID_W)
    col_start = jnp.clip(col - NA_WIN_C // 2, 0, GRID_W - NA_WIN_C)
    col_ok = (col[None, :] >= col_start[:, None]) & (col[None, :] < col_start[:, None] + NA_WIN_C)
    qg = q.reshape(B, rows, GRID_W, H, Dh)
    kg = k.reshape(B, rows, GRID_W, H, Dh)[:, key_rows]
    vg = v.reshape(B, rows, GRID_W, H, Dh)[:, key_rows]
    scale = Dh ** -0.5
    s_loc = jnp.einsum('brqhd,brjkhd->brhqjk', qg, kg).astype(jnp.float32) * scale
    d_row = key_rows - r_idx[:, None] + (NA_WIN_R - 1)
    d_col = jnp.clip(col[None, :] - col[:, None] + (NA_WIN_C - 1), 0, 2 * NA_WIN_C - 2)
    bias = rpb[:, d_row[:, None, :, None], d_col[None, :, None, :]]
    s_loc = s_loc + jnp.moveaxis(bias, 0, 1)[None].astype(jnp.float32)
    s_loc = jnp.where(col_ok[:, None, :], s_loc, NEG_INF).reshape(B, rows, H, GRID_W, wr * GRID_W)
    s_ctx = jnp.einsum('brqhd,bkhd->brhqk', qg, k_ctx).astype(jnp.float32) * scale
    p = jax.nn.softmax(jnp.concatenate([s_loc, s_ctx], axis=-1), axis=-1).astype(q.dtype)
    p_loc = p[..., :wr * GRID_W].reshape(B, rows, H, GRID_W, wr, GRID_W)
    p_ctx = p[..., wr * GRID_W:]
    out = jnp.einsum('brhqjk,brjkhd->brqhd', p_loc, vg) + jnp.einsum('brhqk,bkhd->brqhd', p_ctx, v_ctx)
    return out.reshape(B, L, H * Dh)

def context_attention(q, k, v):
    B, C, H, Dh = q.shape
    s = jnp.einsum('bqhd,bkhd->bhqk', q, k).astype(jnp.float32) * (Dh ** -0.5)
    p = jax.nn.softmax(s, axis=-1).astype(q.dtype)
    return jnp.einsum('bhqk,bkhd->bqhd', p, v).reshape(B, C, H * Dh)

def merge_branches(h, ys, w_branch, w_gate, w_out):
    merged = jax.nn.sigmoid(h @ w_gate[:, 0]) * (ys[0] @ w_branch[0])
    for n in range(1, N_BRANCH):
        merged = merged + jax.nn.sigmoid(h @ w_gate[:, n]) * (ys[n] @ w_branch[n])
    return merged @ w_out

def swiglu(h, w_g, w_u, w_d):
    return (jax.nn.silu(h @ w_g) * (h @ w_u)) @ w_d

def setup_inputs(seed: int = 0) -> dict:
    key = jax.random.key(seed)
    ks = jax.random.split(key, 32)
    f32 = jnp.float32
    D = D_MODEL

    def nrm(k, shape, std):
        return jax.random.normal(k, shape, f32) * std

    a_c = jax.random.uniform(ks[21], (DEPTH, 2, BRANCH_W), f32, 0.9, 0.999)
    a_base = a_c ** (1.0 / LRU_C)
    return {
        "x": nrm(ks[0], (BATCH, SEQ, D), 1.0),
        "c": nrm(ks[1], (BATCH, D), 1.0),
        "ctx": nrm(ks[2], (BATCH, CTX_LEN, D), 1.0),
        "c_ctx": nrm(ks[3], (D,), 1.0),
        "w_mod": nrm(ks[4], (DEPTH, D, 6 * D), 0.5 * D ** -0.5),
        "b_mod": nrm(ks[5], (DEPTH, 6 * D), 0.02),
        "g_mix": 1.0 + nrm(ks[6], (DEPTH, D), 0.02),
        "g_ffn": 1.0 + nrm(ks[7], (DEPTH, D), 0.02),
        "g_final": 1.0 + nrm(ks[8], (D,), 0.02),
        "w_in": nrm(ks[9], (DEPTH, D, IN_W), D ** -0.5),
        "w_pool": nrm(ks[10], (DEPTH, N_GROUPS, GROUP_W, GROUP_W), GROUP_W ** -0.5),
        "pool_scale": 1.0 + nrm(ks[11], (DEPTH, BRANCH_W), 0.1),
        "gmlp_ln_g": 1.0 + nrm(ks[12], (DEPTH, BRANCH_W), 0.02),
        "w_sp": nrm(ks[13], (DEPTH, N_GROUPS, CHUNK, CHUNK), CHUNK ** -0.5),
        "b_sp": 1.0 + nrm(ks[14], (DEPTH, N_GROUPS, CHUNK), 0.1),
        "conv_w": nrm(ks[15], (DEPTH, CONV_W, BRANCH_W), CONV_W ** -0.5),
        "conv_b": nrm(ks[16], (DEPTH, BRANCH_W), 0.02),
        "w_rg": nrm(ks[17], (DEPTH, 2, N_GROUPS, GROUP_W, GROUP_W), GROUP_W ** -0.5),
        "b_rg": nrm(ks[18], (DEPTH, 2, BRANCH_W), 0.1),
        "w_ig": nrm(ks[19], (DEPTH, 2, N_GROUPS, GROUP_W, GROUP_W), GROUP_W ** -0.5),
        "b_ig": nrm(ks[20], (DEPTH, 2, BRANCH_W), 0.1),
        "lru_lam": jnp.log(a_base) - jnp.log1p(-a_base),
        "rpb": nrm(ks[22], (DEPTH, NA_HEADS, 2 * NA_WIN_R - 1, 2 * NA_WIN_C - 1), 0.1),
        "w_branch": nrm(ks[23], (DEPTH, N_BRANCH, BRANCH_W, D), BRANCH_W ** -0.5),
        "w_gate": nrm(ks[24], (DEPTH, D, N_BRANCH, D), D ** -0.5),
        "w_out": nrm(ks[25], (DEPTH, D, D), D ** -0.5),
        "w_ffn_gate": nrm(ks[26], (DEPTH, D, D_FF), D ** -0.5),
        "w_ffn_up": nrm(ks[27], (DEPTH, D, D_FF), D ** -0.5),
        "w_ffn_down": nrm(ks[28], (DEPTH, D_FF, D), D_FF ** -0.5),
    }

def reference(x, c, ctx, c_ctx, w_mod, b_mod, g_mix, g_ffn, g_final, w_in, w_pool, pool_scale,
              gmlp_ln_g, w_sp, b_sp, conv_w, conv_b, w_rg, b_rg, w_ig, b_ig, lru_lam, rpb,
              w_branch, w_gate, w_out, w_ffn_gate, w_ffn_up, w_ffn_down):
    B = x.shape[0]
    for l in range(DEPTH):
        last = l == DEPTH - 1
        sh1, sc1, gt1, sh2, sc2, gt2 = adaln(c, w_mod[l], b_mod[l])
        csh1, csc1, cgt1, csh2, csc2, cgt2 = adaln(c_ctx, w_mod[l], b_mod[l])

        hx = modulate(rms_norm(x, g_mix[l]), sh1, sc1)
        hc = modulate(rms_norm(ctx, g_mix[l]), csh1, csc1)
        x_pool, x_u, x_v, x_lru, x_lg, x_q, x_k, x_val = jnp.split(hx @ w_in[l], N_IN_SLICES, axis=-1)
        c_pool, c_u, c_v, c_lru, c_lg, c_q, c_k, c_val = jnp.split(hc @ w_in[l], N_IN_SLICES, axis=-1)

        k_ctx, v_ctx = heads(c_k), heads(c_val)
        c_conv = centred_depthwise_conv(c_lru, conv_w[l], conv_b[l])
        h_zero = jnp.zeros((B, BRANCH_W), jnp.float32)
        hc_f = rg_lru(c_conv, w_rg[l, 0], b_rg[l, 0], w_ig[l, 0], b_ig[l, 0], lru_lam[l, 0], h_zero, False)
        hc_b = rg_lru(c_conv, w_rg[l, 1], b_rg[l, 1], w_ig[l, 1], b_ig[l, 1], lru_lam[l, 1], h_zero, True)

        y_pool = pool_branch(x_pool, w_pool[l], pool_scale[l])
        y_sgu = spatial_gating(x_u, x_v, gmlp_ln_g[l], w_sp[l], b_sp[l])
        x_conv = centred_depthwise_conv(x_lru, conv_w[l], conv_b[l])
        hx_f = rg_lru(x_conv, w_rg[l, 0], b_rg[l, 0], w_ig[l, 0], b_ig[l, 0], lru_lam[l, 0], hc_f[:, -1], False)
        hx_b = rg_lru(x_conv, w_rg[l, 1], b_rg[l, 1], w_ig[l, 1], b_ig[l, 1], lru_lam[l, 1], hc_b[:, 0], True)
        y_lru = (hx_f + hx_b).astype(x.dtype) * jax.nn.gelu(x_lg)
        y_na = neighbourhood_attention(heads(x_q), heads(x_k), heads(x_val), k_ctx, v_ctx, rpb[l])
        x_mixed = x + gt1 * merge_branches(hx, [y_pool, y_sgu, y_lru, y_na], w_branch[l], w_gate[l], w_out[l])

        if not last:
            yc_pool = pool_branch(c_pool, w_pool[l], pool_scale[l])
            yc_sgu = spatial_gating(c_u, c_v, gmlp_ln_g[l], w_sp[l], b_sp[l])
            yc_lru = (hc_f + hc_b).astype(ctx.dtype) * jax.nn.gelu(c_lg)
            yc_na = context_attention(heads(c_q), k_ctx, v_ctx)
            ctx = ctx + cgt1 * merge_branches(hc, [yc_pool, yc_sgu, yc_lru, yc_na], w_branch[l], w_gate[l], w_out[l])
            hc2 = modulate(rms_norm(ctx, g_ffn[l]), csh2, csc2)
            ctx = ctx + cgt2 * swiglu(hc2, w_ffn_gate[l], w_ffn_up[l], w_ffn_down[l])

        hx2 = modulate(rms_norm(x_mixed, g_ffn[l]), sh2, sc2)
        x = x_mixed + gt2 * swiglu(hx2, w_ffn_gate[l], w_ffn_up[l], w_ffn_down[l])
    return rms_norm(x, g_final)


_drawn_inputs = setup_inputs


def setup_inputs(seed=0):
    import zlib

    import numpy as np

    out = dict(_drawn_inputs(seed))
    spreads = {}
    factors = {'g_mix': 5.79,
     'g_ffn': 33.597,
     'g_final': 23.021,
     'pool_scale': 14.576,
     'gmlp_ln_g': 67.16,
     'b_sp': 14.015,
     'b_rg': 23.971,
     'b_ig': 20.673,
     'rpb': 200.0,
     'conv_b': 10.387}
    for name, (base, spread) in spreads.items():
        noise = np.random.default_rng([zlib.crc32(name.encode()), seed]).standard_normal(out[name].shape)
        drawn = base * np.exp(spread * noise) if base else spread * noise
        out[name] = __import__('jax').numpy.asarray(drawn.astype(out[name].dtype))
    for name, factor in factors.items():
        out[name] = (out[name] * factor).astype(out[name].dtype)
    return out
```

```python
from contextlib import ExitStack

import numpy as np

import concourse.bass as bass
from concourse import mybir

F32 = mybir.dt.float32
F32R = mybir.dt.float32r
ALU = mybir.AluOpType
ACT = mybir.ActivationFunctionType
AX_X = mybir.AxisListType.X

P = 128
D = 2048
T = 256
KT = D // P
BW = 512
G4 = BW // P
NB = 4
DFF = 5632
FC = DFF // BW
RING = 4
PC = 2 * BW
GRID = 64
WIN_R, WIN_C = 8, 16
POOL_WINDOWS = (2, 4, 8, 16)
PAD = 8
ZW = T + 2 * PAD
CONV = 4
LW = T + CONV
EPS = 1e-6
MASKED = -1e30
NDR = 7
PITCH = 128

MOD0 = 0
WIN0 = MOD0 + 8 * 8
MIX0 = WIN0 + 8 * 8
BLK = NB * 8 + NB * 2
OUT0 = MIX0 + 4 * BLK
FFN0 = OUT0 + 4 * 8
LOOP0 = FFN0 + 16
LAST0 = LOOP0 + (FC - 1) * 24

S_POOL, S_U, S_V, S_LRU, S_LG, S_Q, S_K, S_VAL = range(8)
WIN_ORDER = (S_K, S_VAL, S_Q, S_LRU, S_POOL, S_V, S_U, S_LG)

PA_BMOD, PA_GMIX, PA_GFFN = 0, 96, 112
PB_C, PB_CC, PB_PS, PB_CW, PB_CB, PB_BR, PB_BI, PB_LAM, PB_GF = 0, 16, 32, 36, 52, 56, 64, 72, 80
PB_N = 96
CST_MASK, CST_SEL, CST_N = 128, 192, 194

ATT_A, ATT_B = 36, 54
LRU_STEP = 5
LRU_0 = 77


class Own:

    def __init__(self, eng, sem):
        self.eng, self.sem, self.n, self.i, self.per = eng, sem, 0, None, 0

    def did(self, ins):
        ins.then_inc(self.sem, 1)
        self.n += 1
        return ins

    def wait(self, back=0):
        n = self.n - back
        self.eng.wait_ge(self.sem, n if self.i is None else n + self.i * self.per)

    def enter(self, i, first, per):
        self.i, self.per, self.n0 = i, per, self.n
        self.n -= first * per

    def leave(self, first, count):
        assert self.n + first * self.per - self.n0 == self.per, (self.n + first * self.per - self.n0, self.per)
        self.i = None
        self.n = self.n0 + count * self.per


def build(nc, x, c, ctx, c_ctx, w_mod, b_mod, g_mix, g_ffn, g_final, w_in, w_pool, pool_scale,
          gmlp_ln_g, w_sp, b_sp, conv_w, conv_b, w_rg, b_rg, w_ig, b_ig, lru_lam, rpb,
          w_branch, w_gate, w_out, w_ffn_gate, w_ffn_up, w_ffn_down, cst, rc, out):
    ctxs = ExitStack()
    with ctxs:
        def sb(name, shape, dt=F32):
            return ctxs.enter_context(nc.sbuf_tensor(name, shape, dt))

        def sem(name):
            return ctxs.enter_context(nc.semaphore(name))

        RAW = sb("RAW", [P, RING, PC])
        HI = sb("HI", [P, RING, PC], F32R)
        LO = sb("LO", [P, RING, PC], F32R)
        H = sb("H", [P, 2, KT, 2, T], F32R)
        HX = H[:, 1, :, :, :]
        Y = H[:, 0, :, :, :]
        HID = H[:, 0, 0:G4, :, :]
        SC = sb("SC", [P, KT, 4], F32R)
        SCF = sb("SCF", [P, 2, KT])
        CST = sb("CST", [P, CST_N])
        IDENT = CST[:, 0:P]
        PA = sb("PA", [P, P])
        PB = sb("PB", [P, PB_N])
        MC1 = sb("MC1", [P, 2 * KT, 2])
        A1 = sb("A1", [P, KT, 2])
        MC2 = sb("MC2", [P, 4 * KT])
        A2 = sb("A2", [P, KT])
        ONES = sb("ONES", [P, P])
        EPSC = sb("EPSC", [P, 1])
        ST = sb("ST", [P, 64])
        LRC = sb("LRC", [P, 8, 8])
        RSTD = sb("RSTD", [P, T])

        ATT = sb("ATT", [P, 8704])
        XT = ATT[:, 0:8192].rearrange("p (s k t) -> p s k t", s=2, k=KT)
        PAROW = ATT[:, 8192:8320]
        PBROW = ATT[0:PB_N, 8320:8448]
        RP = ATT[0:NB * NDR, 8448:8576]
        KTT = ATT[:, 0:2048].rearrange("p (h t) -> p h t", h=G4)
        VAL = ATT[:, 2048:4096].rearrange("p (s n) -> p s n", s=4)
        QT = ATT[:, 4096:5120].rearrange("p (h t) -> p h t", h=G4)
        TB = ATT[:, 5120:6656].rearrange("p (h j n) -> p h j n", h=G4, j=6)
        PT = ATT[:, 6656:8704].rearrange("p (h j t) -> p h j t", h=2, j=4)
        S4 = ATT[:, 0:4096].rearrange("p (n e) -> p n e", n=NB)
        MG = ATT[:, 4096:8192].rearrange("p (f e) -> p f e", f=4)
        LT = ATT[:, 4096:8192].rearrange("p (u a e) -> p u a e", u=2, a=4)
        ACC = ATT[:, 0:4096].rearrange("p (n e) -> p n e", n=4)
        SG = ATT[:, 4096:5120]
        TG = ATT[:, 5120:6144]
        HD = ATT[:, 6144:7168]

        BR = sb("BR", [P, 13152])
        XTOK = BR[:, 0:8192].rearrange("p (s n) -> p s n", s=4)
        MROW = BR[0:4, 8192:12288]
        LP = BR[:, 0:2080].rearrange("p (g s w) -> p g s w", g=G4, s=2)
        LG = BR[:, 2080:3104]
        RC = BR[:, 2080:3104].rearrange("p (g t) -> p g t", g=G4)
        U = BR[:, 3104:4128].rearrange("p (g t) -> p g t", g=G4)
        V = BR[:, 4128:5152].rearrange("p (s n) -> p s n", s=2)
        ZP = BR[:, 5152:6240].rearrange("p (g w) -> p g w", g=G4)
        Z = BR[:, 6240:7264].rearrange("p (b e) -> p b e", b=2)
        YF = BR[:, 7264:8288].rearrange("p (g t) -> p g t", g=G4)
        PR = BR[:, 6240:8288].rearrange("p (u e) -> p u e", u=4)
        SW = BR[:, 8288:11360].rearrange("p (m n) -> p m n", m=24)
        WSPT = BR[:, 11360:11872].rearrange("p (g n) -> p g n", g=G4)
        LNG = BR[:, 11872:12384]
        BSP = BR[:, 12384:12896]
        HS = BR[:, 12896:13152]
        XT2 = BR[:, 0:4096].rearrange("p (s n) -> p s n", s=2)
        ACCG = BR[:, 0:2048].rearrange("p (m n) -> p m n", m=4)
        XM = BR[:, 4096:8192].rearrange("p (k t) -> p k t", k=KT)
        MR = BR[:, 8192:10240].rearrange("p (s e) -> p s e", s=2)
        ACCM = BR[:, 10240:11264].rearrange("p (s e) -> p s e", s=2)
        SQ = BR[:, 11264:12288]
        OTOK = ATT[:, 4096:8192].rearrange("p (s n) -> p s n", s=2)

        ps = ctxs.enter_context(nc.psum_tensor("ps", [P, 8, BW], F32))

        def pair(b):
            return ps[:, b:b + 2, :]

        def flat(ap):
            return ap.rearrange("p (b e) -> p b e", b=2)

        toeplitz = nc.dram_tensor("toeplitz_rows", [NB * NDR * GRID * PITCH], F32, kind="Internal").ap()

        landed = [sem(f"piece_landed{s}") for s in range(RING)]
        hi_done = sem("hi_done")
        lo_done = sem("lo_done")
        used = sem("piece_used")
        own_a, own_v = sem("act_own"), sem("dve_own")
        S = {}

        def s(name):
            if name not in S:
                S[name] = sem(name)
            return S[name]

        def view(w):
            return w.rearrange("(q t p) n -> p q t n", t=2, p=P)

        v_mod, v_in, v_out = view(w_mod[0]), view(w_in[0]), view(w_out[0])
        v_gate = w_gate[0].rearrange("(q t p) b n -> p q t (b n)", t=2, p=P)
        v_branch = w_branch[0].rearrange("b (q t p) n -> p (b q) t n", t=2, p=P)
        v_fg, v_fu, v_fd = view(w_ffn_gate[0]), view(w_ffn_up[0]), view(w_ffn_down[0])

        block = ctxs.enter_context(nc.Block())

        @block.sync
        def _(sp):
            def piece(p, j, view, q, col):
                sp.wait_ge(lo_done, p + 1)
                sp.dma_start(RAW[:, j % RING, :].rearrange("p (t n) -> p t n", t=2),
                             view[:, q, :, bass.ds(col, BW)]).then_inc(landed[j % RING], 16)

            for k, src in enumerate((ctx[0, 0:P, :], ctx[0, P:T, :], x[0, 0:P, :], x[0, P:T, :])):
                sp.dma_start(XTOK[:, k, :], src).then_inc(s(f"tokens{k}"), 16)
            with sp.Fori(0, 8) as n:
                for j in range(8):
                    piece(n * 8 + j, j, v_mod, j, n * BW)
            for n, sl in enumerate(WIN_ORDER):
                for j in range(8):
                    piece(WIN0 + 8 * n + j, j, v_in, j, sl * BW)

            def gates(f, base):
                with sp.Fori(0, NB) as n:
                    for j in range(8):
                        piece(base + n * 8 + j, j, v_gate, j, n * D + f * BW)

            def branches(f, base):
                for j in range(8):
                    piece(base + 32 + j, j, v_branch, j, f * BW)

            with sp.Fori(0, 4) as f:
                gates(f, MIX0 + f * BLK)
                branches(f, MIX0 + f * BLK)
            with sp.Fori(0, 4) as n:
                for j in range(8):
                    piece(OUT0 + n * 8 + j, j, v_out, j, n * BW)
            for j in range(8):
                piece(FFN0 + j, j, v_fg, j, 0)
            for j in range(8):
                piece(FFN0 + 8 + j, j, v_fu, j, 0)
            with sp.Fori(1, FC) as m:
                base = LOOP0 - 24 + m * 24
                for j in range(8):
                    piece(base + j, j, v_fg, j, m * BW)
                for j in range(8):
                    sp.wait_ge(lo_done, base + 8 + j + 1)
                    sp.dma_start(RAW[:, j % RING, :].rearrange("p (t n) -> p t n", t=2),
                                 v_fd[:, bass.ds(m * 2 - 2 + j % 2, 1), :, j // 2 * BW:j // 2 * BW + BW])\
                        .then_inc(landed[j % RING], 16)
                for j in range(8):
                    piece(base + 16 + j, j, v_fu, j, m * BW)
            for j in range(8):
                piece(LAST0 + j, j, v_fd, 2 * FC - 2 + j % 2, j // 2 * BW)
            for t in range(2):
                sp.wait_ge(s("out_rows"), 4 * (t + 1))
                sp.dma_start(out[0, t * P:(t + 1) * P, :], OTOK[:, t, :]).then_inc(s(f"stored{t}"), 16)
            for t in range(2):
                sp.wait_ge(s(f"stored{t}"), 16)

        @block.gpsimd
        def _(pool):
            pool.dma_start(CST[:, :], cst).then_inc(s("cst_in"), 16)
            rows = [(PAROW, 0, b_mod[0].rearrange("(a n) -> a n", n=P)),
                    (PAROW, PA_GMIX, g_mix[0].rearrange("(a n) -> a n", n=P)),
                    (PAROW, PA_GFFN, g_ffn[0].rearrange("(a n) -> a n", n=P)),
                    (PBROW, PB_C, c[0].rearrange("(a n) -> a n", n=P)),
                    (PBROW, PB_CC, c_ctx.rearrange("(a n) -> a n", n=P)),
                    (PBROW, PB_PS, pool_scale[0].rearrange("(a n) -> a n", n=P)),
                    (PBROW, PB_CW, conv_w[0].rearrange("k (a n) -> (k a) n", n=P)),
                    (PBROW, PB_CB, conv_b[0].rearrange("(a n) -> a n", n=P)),
                    (PBROW, PB_BR, b_rg[0].rearrange("k (a n) -> (k a) n", n=P)),
                    (PBROW, PB_BI, b_ig[0].rearrange("k (a n) -> (k a) n", n=P)),
                    (PBROW, PB_LAM, lru_lam[0].rearrange("k (a n) -> (k a) n", n=P)),
                    (PBROW, PB_GF, g_final.rearrange("(a n) -> a n", n=P))]
            for dst, r0, src in rows:
                n = src.shape[0]
                pool.dma_start(dst[r0:r0 + n, :], src).then_inc(s("rows_in"), 16)
            pool.wait_ge(s("rp_zero"), 1)
            for h in range(NB):
                pool.dma_start(RP[h * NDR:(h + 1) * NDR, 48:48 + 2 * WIN_C - 1],
                               rpb[0, h, WIN_R - 4:WIN_R - 4 + NDR, :]).then_inc(s("rp_in"), 16)
            pool.wait_ge(s("rp_in"), 16 * NB)
            pool.dma_start(toeplitz.rearrange("(r c m) -> r c m", r=NB * NDR, c=GRID),
                           RP.unsqueeze(1).to_broadcast([NB * NDR, GRID, PITCH])).then_inc(s("toeplitz_out"), 16)
            pool.wait_ge(s("h_free"), 1)
            for i, (m0, src) in enumerate(((0, w_pool[0]), (4, w_sp[0]), (8, w_rg[0].rearrange("a g p n -> (a g) p n")),
                                           (16, w_ig[0].rearrange("a g p n -> (a g) p n")))):
                n = src.shape[0]
                pool.dma_start(SW[:, m0:m0 + n, :], src.rearrange("m p n -> p m n")).then_inc(s("small_in"), 16)
            pool.dma_start(LNG, gmlp_ln_g.to_broadcast([P, BW])).then_inc(s("small_in"), 16)
            pool.dma_start(BSP, b_sp.rearrange("a g n -> a (g n)").to_broadcast([P, BW])).then_inc(s("small_in"), 16)
            pool.dma_start(RC.rearrange("p g t -> p (g t)"), rc.rearrange("(a n) -> a n", a=1).to_broadcast([P, 4 * T]))\
                .then_inc(s("small_in"), 16)
            pool.wait_ge(s("toeplitz_out"), 16)
            for half in range(2):
                for h in range(NB):
                    src = bass.AP(toeplitz.tensor, (h * NDR + 1 - half) * GRID * PITCH + GRID - 1,
                                  [[PITCH - 1, GRID], [GRID * PITCH, 6], [1, GRID]])
                    pool.dma_start(TB[half * GRID:(half + 1) * GRID, h, :, :], src).then_inc(s("tb_in"), 16)
            def mod_piece(r, j, m):
                pool.wait_ge(s("mod_used"), r + 1)
                pool.dma_start(MR[:, j % 2, :].rearrange("p (t n) -> p t n", t=2),
                               v_mod[:, j, :, bass.ds(2 * D + m * BW, BW)]).then_inc(s(f"mod_landed{j % 2}"), 16)

            pool.wait_ge(s("branches_made"), 1)
            for t in range(2):
                pool.dma_start(XT2[:, t, :], x[0, t * P:(t + 1) * P, :]).then_inc(s("x_again"), 16)
            with pool.Fori(0, 16) as m:
                for j in range(8):
                    mod_piece(m * 8 + j, j, m)

        @block.scalar
        def _(act):
            own = Own(act, own_a)

            def high(base4, j):
                act.wait_ge(landed[j % RING], base4 * 16 + 16 * (j // 4 + 1))
                act.wait_ge(used, base4 * 4 + j + 1)
                act.activation(HI[:, j % RING, :], RAW[:, j % RING, :], ACT.Copy).then_inc(hi_done, 1)

            act.wait_ge(s("consts_set"), 1)
            for k in range(4):
                act.wait_ge(s(f"tokens{k}"), 16)
                act.activation(ATT[:, k * D:(k + 1) * D], XTOK[:, k, :], ACT.Square, accum_out=ST[:, k:k + 1])\
                    .then_inc(s("ssq"), 1)
            act.wait_ge(s("ssq"), 4)
            act.activation(ST[:, 4:8], ST[:, 0:4], ACT.Sqrt, bias=EPSC[:, 0:1], scale=1.0 / D).then_inc(s("rms"), 1)
            act.wait_ge(s("params"), 1)
            act.activation(LRC[:, 0, :], PB[:, PB_LAM:PB_LAM + 8], ACT.Abs).then_inc(own_a, 1)
            act.activation(ST[:, 16:48], PB[:, PB_C:PB_C + 32], ACT.Sigmoid).then_inc(s("sigc"), 1)
            own.n = 1
            own.wait()
            act.activation(LRC[:, 1, :], LRC[:, 0, :], ACT.Exp, scale=-1.0).then_inc(s("explam"), 1)
            act.wait_ge(s("siluc"), 1)
            act.activation(SC[:, :, 0:2], SCF[:, :, :].rearrange("p w k -> p k w"), ACT.Copy).then_inc(s("sc_hi"), 1)
            for b in range(0, 16, 2):
                act.wait_ge(s("x_turned"), b + 1)
                act.activation(XT[:, b // 8, b % 4 * 4:b % 4 * 4 + 4, b // 4 % 2 * P:b // 4 % 2 * P + P],
                               ps[:, b % 8, :].rearrange("p (k t) -> p k t", k=4), ACT.Copy).then_inc(s("xt_act"), 1)
            with act.Fori(0, 8) as n:
                for j in range(8):
                    high(n * 2, j)
            for q in range(8):
                act.wait_ge(s("h_float"), q + 1)
                act.activation(H[:, :, 2 * q:2 * q + 2, 0, :], XT[:, :, 2 * q:2 * q + 2, :], ACT.Copy).then_inc(s("h_hi"), 1)

            def evac_win(n):
                act.wait_ge(used, WIN0 + 8 * n + 8 + 4)
                sl = WIN_ORDER[n]
                if sl in (S_K, S_VAL, S_Q) and n < 2:
                    act.wait_ge(s("h_lo"), 8)
                if sl == S_K:
                    i = act.activation(KTT, ps[:, 0:4, :], ACT.Copy)
                elif sl == S_VAL:
                    i = act.activation(VAL, ps[:, 4:8, :], ACT.Copy)
                elif sl == S_Q:
                    i = act.activation(flat(ATT[:, 4096:5120]), pair(0), ACT.Copy, scale=float(P) ** -0.5)
                elif sl == S_LRU:
                    for g in range(G4):
                        i = act.activation(LP[:, g, :, 2:2 + T], ps[:, 4 + g, :].rearrange("p (s t) -> p s t", s=2), ACT.Copy)
                elif sl == S_POOL:
                    for b in range(2):
                        i = act.activation(ZP[:, 2 * b:2 * b + 2, PAD:PAD + T],
                                           ps[:, b, :].rearrange("p (g t) -> p g t", g=2), ACT.Copy)
                elif sl == S_V:
                    i = act.activation(V, pair(2), ACT.Copy)
                elif sl == S_U:
                    i = act.activation(flat(BR[:, 3104:4128]), pair(0), ACT.Copy)
                else:
                    act.wait_ge(s("pooled"), 1)
                    i = act.activation(flat(LG), pair(2), ACT.Copy)
                i.then_inc(s("win_read"), 1)

            def gate(f, n, b):
                act.wait_ge(used, f * BLK + (MIX0 + 8 * n + 8 + 4))
                if f != 0 if isinstance(f, int) else True:
                    act.wait_ge(s("merge_add"), f * 4 + (n + 1 - 4))
                elif n == 0:
                    act.wait_ge(s("att_out"), 4)
                elif n == 3:
                    act.wait_ge(s("gelu_made"), 1)
                act.activation(flat(S4[:, n, :]), pair(b), ACT.Sigmoid).then_inc(s("gate_read"), 1)

            def straight(w):
                if w % 8 == 3 and 8 < w < 68:
                    evac_win(w // 8 - 1)
                if w == 22:
                    act.wait_ge(s("wsp_turned"), 1)
                    act.activation(flat(BR[:, 11360:11872])[:, :, :], ps[:, 2, :].rearrange("p (b e) -> p b e", b=2), ACT.Copy)\
                        .then_inc(s("wspt"), 1)
                if w == 63:
                    act.wait_ge(s("v_stats"), 1)
                    act.activation(ST[:, 32:34], ST[:, 28:32].rearrange("p (t e) -> p t e", e=2)[:, :, 1], ACT.Sqrt,
                                   bias=EPSC[:, 0:1]).then_inc(s("v_std"), 1)
                for half, w0 in enumerate((ATT_A, ATT_B)):
                    if w == w0 + 4:
                        for u in range(4):
                            act.wait_ge(s("row_max"), 4 * half + u + 1)
                            act.activation(PR[:, u, :], ps[:, 4 + u, :], ACT.Exp, bias=ST[:, 8 + u:9 + u],
                                           accum_out=ST[:, 12 + u:13 + u]).then_inc(s("exps"), 1)
                    if w == w0 + 11:
                        for u in range(4):
                            act.wait_ge(s("p_turned"), 4 * half + u + 1)
                            if half:
                                act.wait_ge(s("att_av"), 2)
                            act.activation(PT[:, u // 2, :, u % 2 * P:u % 2 * P + P],
                                           ps[:, 4 + u, :].rearrange("p (j t) -> p j t", j=4), ACT.Copy).then_inc(s("pt"), 1)
                    if w == w0 + 16:
                        for hh in range(2):
                            act.wait_ge(s("att_av"), 2 * half + hh + 1)
                            act.wait_ge(s("h_last_read"), 1)
                            act.activation(Y[:, 12 + 2 * half + hh, 0, :], ps[:, 4 + 2 * hh, 0:T], ACT.Copy).then_inc(s("att_hi"), 1)
                if w == 76:
                    act.wait_ge(s("pool_mm"), 1)
                    for g in range(G4):
                        act.activation(Y[:, g, 0, :], ps[:, 4 + g // 2, g % 2 * T:g % 2 * T + T], ACT.Copy,
                                       scale=PB[:, PB_PS + g:PB_PS + g + 1]).then_inc(s("pool_hi"), 1)
                    act.wait_ge(s("sgu_float"), 1)
                    act.activation(Y[:, 4:8, 0, :], YF, ACT.Copy).then_inc(s("sgu_hi"), 1)
                if w == 70:
                    act.wait_ge(s("gelu_arg"), 1)
                    act.activation(S4[:, 3, :], S4[:, 3, :], ACT.Sigmoid, scale=2.0 * (2.0 / np.pi) ** 0.5).then_inc(s("gelu_sig"), 1)
                for g in range(G4):
                    if w == LRU_0 + LRU_STEP * g + 4:
                        for d in range(2):
                            n = 2 * g + d
                            act.wait_ge(s("lru_mm"), n + 1)
                            if g:
                                act.wait_ge(s("lru_scan"), 2 * g - 1 + d)
                            else:
                                act.wait_ge(s("att_out"), 4)
                            col = d * 4 + g
                            act.activation(LT[:, d, 0, :], ps[:, 4 + 2 * d, :], ACT.Sigmoid, bias=PB[:, PB_BR + col:PB_BR + col + 1]).then_inc(s("lru_r"), 1)
                            act.activation(LT[:, d, 1, :], ps[:, 5 + 2 * d, :], ACT.Sigmoid, bias=PB[:, PB_BI + col:PB_BI + col + 1]).then_inc(s("lru_i"), 1)
                        for d in range(2):
                            n = 2 * g + d
                            col = d * 4 + g
                            act.wait_ge(s("lru_r"), n + 1)
                            act.activation(LT[:, d, 2, :], LT[:, d, 0, :], ACT.Tanh, scale=LRC[:, 6, col:col + 1]).then_inc(s("lru_t"), 1)
                            act.activation(LT[:, d, 3, :], LT[:, d, 0, :], ACT.Exp, scale=LRC[:, 7, col:col + 1]).then_inc(s("lru_e"), 1)
                        for d in range(2):
                            act.wait_ge(s("lru_w"), 2 * g + d + 1)
                            act.activation(LT[:, d, 3, :], LT[:, d, 3, :], ACT.Sqrt, scale=4.0).then_inc(s("lru_s"), 1)
                        act.wait_ge(s("lru_float"), g + 1)
                        act.activation(Y[:, 8 + g, 0, :], HS, ACT.Copy).then_inc(s("lru_hi"), 1)
                if w in (75, 83, 91, 99):
                    gate(0, (w - 75) // 8, 2 * ((w - 75) // 8 % 2))

            for w in range(104):
                high((WIN0 + w) // 4, w % 4)
                straight(w)

            with act.Fori(1, 4) as f:
                for w in range(BLK):
                    high(f * (BLK // 4) + (MIX0 + w) // 4, w % 4)
                    if w in (11, 19, 27, 35):
                        n = (w - 11) // 8
                        gate(f, n, 2 * (n % 2))

            def merged_high(f):
                act.wait_ge(s("merge_add"), 4 * f + 4)
                act.wait_ge(used, MIX0 + 3 * BLK + 32 + 4)
                act.activation(HX[:, 4 * f:4 * f + 4, 0, :], MG[:, f, :].rearrange("p (k t) -> p k t", k=4), ACT.Copy)\
                    .then_inc(s("mg_hi"), 1)

            for f in range(4):
                merged_high(f)
            for b in range(8):
                act.wait_ge(s("x_turned_again"), b + 1)
                act.activation(XM[:, b % 4 * 4:b % 4 * 4 + 4, b // 4 * P:b // 4 * P + P],
                               ps[:, 4 + b % 4, :].rearrange("p (k t) -> p k t", k=4), ACT.Copy).then_inc(s("xm_set"), 1)

            def square(n):
                act.wait_ge(s("xm_new"), n + 1)
                if n:
                    act.wait_ge(s("sq_used"), n)
                act.activation(SQ, XM[:, 4 * n:4 * n + 4, :], ACT.Square).then_inc(s("sq"), 1)

            for n in range(4):
                for j in range(8):
                    high((OUT0 + 8 * n) // 4, j)
                    if n and j == 5:
                        square(n - 1)
            square(3)
            act.wait_ge(s("sq_used"), 4)
            act.activation(RSTD[:, :], ps[:, 6, 0:T], ACT.Sqrt, bias=EPSC[:, 0:1], scale=1.0 / D).then_inc(s("rms2"), 1)
            for q in range(8):
                act.wait_ge(s("h2_float"), q + 1)
                act.activation(HX[:, 2 * q:2 * q + 2, 0, :], flat(MG[:, q // 2, q % 2 * 512:q % 2 * 512 + 512]), ACT.Copy)\
                    .then_inc(s("h2_hi"), 1)

            def ffn_gate(m, last):
                act.wait_ge(used, last + 1 + 4)
                if not (isinstance(m, int) and m == 0):
                    act.wait_ge(s("ffn_gate_read"), m)
                else:
                    act.wait_ge(s("h2_lo"), 8)
                act.activation(flat(SG), pair(0), ACT.Sigmoid).then_inc(s("ffn_sig"), 1)

            def hidden_high(m):
                act.wait_ge(s("hid_float"), m + 1)
                act.activation(HID[:, :, 0, :], HD.rearrange("p (k t) -> p k t", k=4), ACT.Copy).then_inc(s("hid_hi"), 1)

            for w in range(16):
                high(FFN0 // 4, w)
                if w == 11:
                    ffn_gate(0, FFN0 + 7)
            with act.Fori(1, FC) as m:
                base = LOOP0 - 24 + m * 24
                for w in range(24):
                    high((LOOP0 - 24) // 4 + m * 6, w)
                    if w == 4:
                        hidden_high(m - 1)
                    if w == 11:
                        ffn_gate(m, base + 7)
            for w in range(8):
                high(LAST0 // 4, w)
                if w == 3:
                    hidden_high(FC - 1)

            for n in range(4):
                act.wait_ge(s("xf_new"), n + 1)
                act.wait_ge(s("sq_used"), 4 + n)
                act.activation(SQ, XM[:, 4 * n:4 * n + 4, :], ACT.Square).then_inc(s("sqf"), 1)
            act.wait_ge(s("sq_used"), 8)
            act.activation(RSTD[:, :], ps[:, 6, 0:T], ACT.Sqrt, bias=EPSC[:, 0:1], scale=1.0 / D).then_inc(s("rms3"), 1)
            for b in range(8):
                act.wait_ge(s("y_turned"), b + 1)
                act.activation(OTOK[:, b // 4, b % 4 * BW:b % 4 * BW + BW], ps[:, b % 4, :], ACT.Copy).then_inc(s("out_rows"), 1)

        @block.vector
        def _(dve):
            own = Own(dve, own_v)
            tt, ts, stt = dve.tensor_tensor, dve.tensor_scalar, dve.scalar_tensor_tensor

            def low(p, j):
                dve.wait_ge(hi_done, p + 1)
                tt(LO[:, j % RING, :], RAW[:, j % RING, :], HI[:, j % RING, :], ALU.subtract).then_inc(lo_done, 1)

            dve.memset(EPSC[:, :], EPS).then_inc(lo_done, 1)
            dve.memset(ONES[:, :], 1.0).then_inc(lo_done, 1)
            dve.memset(ST[:, 48:49], 0.0).then_inc(lo_done, 1)
            dve.memset(ST[:, 49:50], 0.0).then_inc(lo_done, 1)
            dve.memset(RP, 0.0).then_inc(s("rp_zero"), 1)
            dve.wait_ge(lo_done, 4)
            dve.memset(ST[:, 50:51], 0.0).then_inc(s("consts_set"), 1)
            dve.wait_ge(s("params_turned"), 1)
            own.did(dve.tensor_copy(PA[:, :], ps[:, 6, 0:P]))
            own.did(dve.tensor_copy(PB[:, :], ps[:, 7, 0:PB_N]))
            own.wait()
            dve.memset(ST[:, 51:52], 0.0).then_inc(s("params"), 1)
            dve.wait_ge(s("sigc"), 1)
            tt(SCF[:, :, :], PB[:, PB_C:PB_C + 32].rearrange("p (w k) -> p w k", w=2),
               ST[:, 16:48].rearrange("p (w k) -> p w k", w=2), ALU.mult).then_inc(s("siluc"), 1)
            dve.wait_ge(s("siluc"), 1)
            dve.wait_ge(s("sc_hi"), 1)
            tt(SC[:, :, 2:4], SCF[:, :, :].rearrange("p w k -> p k w"), SC[:, :, 0:2], ALU.subtract).then_inc(s("sc_lo"), 1)
            dve.wait_ge(s("rms"), 1)
            own.did(dve.reciprocal(ST[:, 4:8], ST[:, 4:8]))
            own.wait()
            for k in range(4):
                ts(XTOK[:, k, :], XTOK[:, k, :], ST[:, 4 + k:5 + k], None, ALU.mult).then_inc(s("rows_scaled"), 1)
            dve.wait_ge(s("explam"), 1)
            own.did(ts(LRC[:, 2, :], LRC[:, 1, :], 2.0, None, ALU.add)); own.wait()
            own.did(dve.reciprocal(LRC[:, 2, :], LRC[:, 2, :])); own.wait()
            own.did(tt(LRC[:, 2, :], LRC[:, 2, :], LRC[:, 1, :], ALU.mult)); own.wait()
            own.did(tt(LRC[:, 3, :], LRC[:, 2, :], LRC[:, 2, :], ALU.mult)); own.wait()
            own.did(ts(LRC[:, 4, :], LRC[:, 3, :], 1.0 / 17, 1.0 / 15, ALU.mult, ALU.add)); own.wait()
            for d in (13, 11, 9, 7, 5, 3, 1):
                own.did(tt(LRC[:, 4, :], LRC[:, 4, :], LRC[:, 3, :], ALU.mult)); own.wait()
                own.did(ts(LRC[:, 4, :], LRC[:, 4, :], 1.0 / d, None, ALU.add)); own.wait()
            own.did(stt(LRC[:, 4, :], LRC[:, 4, :], 2.0, LRC[:, 2, :], ALU.mult, ALU.mult)); own.wait()
            own.did(ts(LRC[:, 5, :], PB[:, PB_LAM:PB_LAM + 8], -1.0, 0.0, ALU.mult, ALU.max)); own.wait()
            own.did(tt(LRC[:, 5, :], LRC[:, 5, :], LRC[:, 4, :], ALU.add)); own.wait()
            own.did(ts(LRC[:, 6, :], LRC[:, 5, :], 4.0, None, ALU.mult))
            own.did(ts(LRC[:, 7, :], LRC[:, 5, :], -8.0, None, ALU.mult))
            for b in range(1, 16, 2):
                dve.wait_ge(s("x_turned"), b + 1)
                dve.tensor_copy(XT[:, b // 8, b % 4 * 4:b % 4 * 4 + 4, b // 4 % 2 * P:b // 4 % 2 * P + P],
                                ps[:, b % 8, :].rearrange("p (k t) -> p k t", k=4)).then_inc(s("xt_dve"), 1)
            with dve.Fori(0, 8) as n:
                for j in range(8):
                    low(n * 8 + j, j)
            dve.wait_ge(used, MOD0 + 64 + 4)
            dve.tensor_copy(MROW.rearrange("p (b e) -> p b e", b=8), ps[0:4, :, :]).then_inc(s("mrow"), 1)
            dve.wait_ge(s("mod1_turned"), 1)
            own.did(tt(MC1[:, :, :], ps[:, 7, 0:64].rearrange("p (j w) -> p j w", w=2),
                       PA[:, PA_BMOD:PA_BMOD + 32].unsqueeze(2).to_broadcast([P, 32, 2]), ALU.add))
            own.wait()
            own.did(stt(A1[:, :, :], MC1[:, KT:2 * KT, :], 1.0,
                        PA[:, PA_GMIX:PA_GMIX + KT].unsqueeze(2).to_broadcast([P, KT, 2]), ALU.add, ALU.mult))
            own.wait()
            dve.wait_ge(s("xt_act"), 8)
            dve.wait_ge(s("xt_dve"), 8)

            def h_low(q):
                dve.wait_ge(s("h_hi"), q + 1)
                tt(H[:, :, 2 * q:2 * q + 2, 1, :], XT[:, :, 2 * q:2 * q + 2, :], H[:, :, 2 * q:2 * q + 2, 0, :],
                   ALU.subtract).then_inc(s("h_lo"), 1)

            for q in range(8):
                for k in (2 * q, 2 * q + 1):
                    for side, w in ((0, 1), (1, 0)):
                        i = ts(XT[:, side, k, :], XT[:, side, k, :], A1[:, k, w:w + 1], MC1[:, k, w:w + 1], ALU.mult, ALU.add)
                i.then_inc(s("h_float"), 1)
                if q:
                    h_low(q - 1)
            h_low(7)
            dve.memset(ST[:, 52:53], 0.0).then_inc(s("h_free"), 1)
            own.did(dve.memset(LP[:, :, :, 0:2], 0.0))
            own.did(dve.memset(LP[:, :, :, 2 + T:LW], 0.0))
            own.did(dve.memset(ZP[:, :, 0:PAD], 0.0))
            own.did(dve.memset(ZP[:, :, PAD + T:ZW], 0.0))

            def split_low(hi_sem, n, lo, src, hi_ap, done):
                dve.wait_ge(s(hi_sem), n)
                tt(lo, src, hi_ap, ALU.subtract).then_inc(s(done), 1)

            def straight(w):
                if w == 30:
                    dve.wait_ge(s("tb_in"), 16 * 8)
                    tt(TB.rearrange("p h j n -> p (h j) n"), TB.rearrange("p h j n -> p (h j) n"),
                       CST[:, CST_MASK:CST_MASK + GRID].unsqueeze(1).to_broadcast([P, 24, GRID]), ALU.add).then_inc(s("tb"), 1)
                for half, w0 in enumerate((ATT_A, ATT_B)):
                    if w == w0 + 4:
                        for u in range(4):
                            dve.wait_ge(s("scores"), 4 * half + u + 1)
                            dve.reduce_max(ST[:, 8 + u:9 + u], ps[:, 4 + u, :], AX_X, negate=True).then_inc(s("row_max"), 1)
                    if w == w0 + 6:
                        for u in range(4):
                            dve.wait_ge(s("exps"), 4 * half + u + 1)
                            own.did(dve.reciprocal(ST[:, 12 + u:13 + u], ST[:, 12 + u:13 + u]))
                        own.wait()
                        for u in range(4):
                            ts(PR[:, u, :], PR[:, u, :], ST[:, 12 + u:13 + u], None, ALU.mult).then_inc(s("probs"), 1)
                    if w == w0 + 17:
                        for hh in range(2):
                            split_low("att_hi", 2 * half + hh + 1, Y[:, 12 + 2 * half + hh, 1, :], ps[:, 4 + 2 * hh, 0:T],
                                      Y[:, 12 + 2 * half + hh, 0, :], "att_out")
                if w == 62:
                    dve.wait_ge(s("win_read"), 6)
                    for t in range(2):
                        own.did(dve.bn_stats(ST[:, 16 + 6 * t:22 + 6 * t], V[:, t, :]))
                    own.wait()
                    for t in range(2):
                        own.did(dve.bn_aggr(ST[:, 28 + 2 * t:30 + 2 * t], ST[:, 16 + 6 * t:22 + 6 * t]))
                    own.wait()
                    dve.memset(ST[:, 53:54], 0.0).then_inc(s("v_stats"), 1)
                if w == 64:
                    dve.wait_ge(s("v_std"), 1)
                    own.did(dve.reciprocal(ST[:, 32:34], ST[:, 32:34])); own.wait()
                    for t in range(2):
                        own.did(ts(V[:, t, :], V[:, t, :], ST[:, 28 + 2 * t:29 + 2 * t], ST[:, 32 + t:33 + t], ALU.subtract, ALU.mult))
                    own.wait()
                    dve.wait_ge(s("small_in"), 16 * 7)
                    for t in range(2):
                        tt(V[:, t, :], V[:, t, :], LNG, ALU.mult).then_inc(s("vn"), 1)
                if w == 65:
                    dve.wait_ge(s("win_read"), 5)
                    dve.wait_ge(s("small_in"), 16 * 7)
                    dve.wait_ge(s("p_turned"), 8)
                    A, B = Z[:, 0, :], Z[:, 1, :]
                    for g, win in enumerate(POOL_WINDOWS):
                        src, o, lo_, hi_ = ZP[:, g, :], 1, 1, ZW
                        dst = A
                        own.did(tt(dst[:, 1:ZW], ZP[:, g, 0:ZW - 1], ZP[:, g, 1:ZW], ALU.add))
                        own.wait()
                        a, b = 1, ZW
                        step = 1
                        cur = dst
                        while 2 * step < win:
                            nxt = B if cur is A else A
                            own.did(tt(nxt[:, a + step:b - step], cur[:, a:b - 2 * step], cur[:, a + 2 * step:b], ALU.add))
                            own.wait()
                            a, b, step, cur = a + step, b - step, 2 * step, nxt
                        own.did(tt(YF[:, g, :], cur[:, PAD:PAD + T], RC[:, g, :], ALU.mult))
                        own.wait()
                    tt(YF, YF, ZP[:, :, PAD:PAD + T], ALU.subtract).then_inc(s("pooled"), 1)
                if w == 69:
                    dve.wait_ge(s("win_read"), 8)
                    dve.wait_ge(s("att_av"), 4)
                    g3 = S4[:, 3, :]
                    own.did(tt(g3, LG, LG, ALU.mult)); own.wait()
                    own.did(ts(g3, g3, 0.044715, 1.0, ALU.mult, ALU.add)); own.wait()
                    tt(g3, g3, LG, ALU.mult).then_inc(s("gelu_arg"), 1)
                if w == 72:
                    dve.wait_ge(s("gelu_sig"), 1)
                    tt(LG, LG, S4[:, 3, :], ALU.mult).then_inc(s("gelu_made"), 1)
                    dve.wait_ge(s("gelu_made"), 1)
                if w == 76:
                    dve.wait_ge(s("pool_mm"), 1)
                    for g in range(G4):
                        if g == 0:
                            dve.wait_ge(s("pool_hi"), 4)
                        stt(Y[:, g, 1, :], ps[:, 4 + g // 2, g % 2 * T:g % 2 * T + T], PB[:, PB_PS + g:PB_PS + g + 1],
                            Y[:, g, 0, :], ALU.mult, ALU.subtract).then_inc(s("pool_lo"), 1)
                if w == 75:
                    dve.wait_ge(s("pool_mm"), 1)
                    dve.wait_ge(s("sgu_mm"), 1)
                    for t in range(2):
                        own.did(tt(YF[:, :, t * P:t * P + P], ps[:, 6 + t, :].rearrange("p (g t) -> p g t", g=4),
                                   BSP.rearrange("p (g t) -> p g t", g=4), ALU.add))
                    own.wait()
                    tt(YF, YF, U, ALU.mult).then_inc(s("sgu_float"), 1)
                if w == 77:
                    split_low("sgu_hi", 1, Y[:, 4:8, 1, :], YF, Y[:, 4:8, 0, :], "sgu_lo")
                for g in range(G4):
                    if w == LRU_0 + LRU_STEP * g + 4:
                        z = Z[:, g % 2, :]
                        for d in range(2):
                            n = 2 * g + d
                            R, I, TH, EA = (LT[:, d, k, :] for k in range(4))
                            dve.wait_ge(s("lru_i"), n + 1)
                            own.did(tt(I, I, z, ALU.mult))
                            dve.wait_ge(s("lru_e"), n + 1)
                            own.did(ts(EA, EA, 1.0, 0.5, ALU.add, ALU.mult)); own.wait()
                            own.did(tt(TH, TH, EA, ALU.mult)); own.wait()
                            own.did(ts(R, TH, -2.0, 1.0, ALU.mult, ALU.add))
                            tt(EA, TH, EA, ALU.mult).then_inc(s("lru_w"), 1)
                        for d in range(2):
                            n = 2 * g + d
                            R, I, TH, EA = (LT[:, d, k, :] for k in range(4))
                            dve.wait_ge(s("lru_s"), n + 1)
                            own.did(tt(I, EA, I, ALU.mult)); own.wait()
                            if d == 0:
                                dve.tensor_tensor_scan(TH, R, I, 0.0, ALU.mult, ALU.add).then_inc(s("lru_scan"), 1)
                            else:
                                own.did(dve.tensor_tensor_scan(TH[:, 0:T][:, ::-1], R[:, 0:T][:, ::-1], I[:, 0:T][:, ::-1],
                                                               0.0, ALU.mult, ALU.add))
                                own.wait()
                                dve.tensor_tensor_scan(TH[:, T:2 * T][:, ::-1], R[:, T:2 * T][:, ::-1], I[:, T:2 * T][:, ::-1],
                                                       TH[:, 0:1], ALU.mult, ALU.add).then_inc(s("lru_scan"), 1)
                        dve.wait_ge(s("lru_scan"), 2 * g + 2)
                        if g:
                            dve.wait_ge(s("lru_lo"), g)
                        own.did(tt(HS, LT[:, 0, 2, T:2 * T], LT[:, 1, 2, T:2 * T], ALU.add)); own.wait()
                        tt(HS, HS, LG[:, g * T:g * T + T], ALU.mult).then_inc(s("lru_float"), 1)
                        split_low("lru_hi", g + 1, Y[:, 8 + g, 1, :], HS, Y[:, 8 + g, 0, :], "lru_lo")
                if w in [71 + LRU_STEP * g for g in range(G4)]:
                    g = (w - 71) // LRU_STEP
                    z = Z[:, g % 2, :].rearrange("p (s t) -> p s t", s=2)
                    dve.wait_ge(s("win_read"), 4)
                    if g == 0:
                        dve.wait_ge(s("pooled"), 1)
                    if g >= 2:
                        dve.wait_ge(s("lru_scan"), 2 * (g - 1))
                    own.did(ts(z, LP[:, g, :, 0:T], PB[:, PB_CW + g:PB_CW + g + 1], PB[:, PB_CB + g:PB_CB + g + 1], ALU.mult, ALU.add))
                    for k in range(1, CONV):
                        own.wait()
                        i = stt(z, LP[:, g, :, k:k + T], PB[:, PB_CW + 4 * k + g:PB_CW + 4 * k + g + 1], z, ALU.mult, ALU.add)
                        if k < CONV - 1:
                            own.did(i)
                        else:
                            i.then_inc(s("conv"), 1)

            def merge(f, n, b):
                dve.wait_ge(used, f * BLK + (MIX0 + 34 + 2 * n + 4))
                dve.wait_ge(s("gate_read"), f * 4 + (n + 1))
                m = flat(MG[:, f, :]) if isinstance(f, int) else MG[:, bass.ds(f, 1), :].rearrange("p o (b e) -> p (o b) e", b=2)
                if n == 0:
                    tt(m, pair(b), flat(S4[:, n, :]), ALU.mult).then_inc(s("merge_read"), 1)
                    dve.wait_ge(s("merge_read"), f * 4 + (n + 1))
                    dve.memset(ST[:, 54:55], 0.0).then_inc(s("merge_add"), 1)
                else:
                    tt(flat(S4[:, n, :]), pair(b), flat(S4[:, n, :]), ALU.mult).then_inc(s("merge_read"), 1)
                    dve.wait_ge(s("merge_read"), f * 4 + (n + 1))
                    dve.wait_ge(s("merge_add"), f * 4 + n)
                    tt(m, m, flat(S4[:, n, :]), ALU.add).then_inc(s("merge_add"), 1)

            for w in range(104):
                low(WIN0 + w, w % 4)
                straight(w)
                if w in (101, 103):
                    merge(0, (w - 101) // 2, (w - 101) % 4)
            dve.wait_ge(s("lru_lo"), 4)
            dve.memset(ST[:, 55:56], 0.0).then_inc(s("mod_used"), 1)
            dve.memset(ST[:, 56:57], 0.0).then_inc(s("mod_used"), 1)
            dve.memset(ST[:, 57:58], 0.0).then_inc(s("branches_made"), 1)

            def mod_piece(r, j, land, acc, first):
                dve.wait_ge(s(f"mod_landed{j % 2}"), land)
                for t in range(2):
                    k = 2 * j + t
                    src, sc = MR[:, j % 2, t * BW:(t + 1) * BW], SCF[:, 0, k:k + 1]
                    if k == 0:
                        i = own.did(ts(acc, src, sc, None, ALU.mult))
                    else:
                        own.wait()
                        i = own.did(stt(acc, src, sc, acc, ALU.mult, ALU.add))
                own.wait()
                dve.memset(ST[:, 58:59], 0.0).then_inc(s("mod_used"), 1)

            def mod_columns(m, n):
                dve.wait_ge(s("mod_summed"), m * 1 + 1)
                own.did(tt(MC2[:, bass.ds(m * 4, 4)], ps[:, 4 + n % 2, 0:4], PA[:, bass.ds(m * 4 + 32, 4)], ALU.add))
                own.wait()

            with dve.Fori(1, 4) as f:
                own.enter(f, 1, 4 * 16 + 4)
                for w in range(BLK):
                    low(f * BLK + (MIX0 + w), w % 4)
                    if w < 32:
                        n, j = w // 8, w % 8
                        mod_piece(None, j, (f - 1) * 256 + (n * 64 + 16 * (j // 2 + 1)), ACCM[:, n % 2, :], j == 0)
                        if j == 7:
                            dve.memset(ST[:, 59:60], 0.0).then_inc(s("acc_made"), 1)
                    if w in (13, 21, 29, 37):
                        n = (w - 13) // 8
                        mod_columns(f * 4 + (n - 4), n)
                    if w == 1:
                        merge(f - 1, 2, 0)
                    if w == 3:
                        merge(f - 1, 3, 2)
                    if w == 37:
                        merge(f, 0, 0)
                    if w == 39:
                        merge(f, 1, 2)
                own.leave(1, 3)

            def merged_low(f):
                split_low("mg_hi", f + 1, HX[:, 4 * f:4 * f + 4, 1, :], MG[:, f, :].rearrange("p (k t) -> p k t", k=4),
                          HX[:, 4 * f:4 * f + 4, 0, :], "mg_lo")

            for f in range(3):
                merged_low(f)
            merge(3, 2, 0)
            merge(3, 3, 2)
            merged_low(3)
            dve.wait_ge(s("xm_set"), 8)
            stt(A2[:, :], MC2[:, 2 * KT:3 * KT], 1.0, PA[:, PA_GFFN:PA_GFFN + KT], ALU.add, ALU.mult).then_inc(s("a2"), 1)

            def residual(n):
                dve.wait_ge(used, OUT0 + 8 * n + 8 + 4)
                for k in range(4):
                    o = pair(2 * (n % 2))[:, k // 2, k % 2 * T:k % 2 * T + T]
                    i = stt(XM[:, 4 * n + k, :], o, MC2[:, 4 * n + k:4 * n + k + 1], XM[:, 4 * n + k, :], ALU.mult, ALU.add)
                i.then_inc(s("xm_new"), 1)

            for n in range(4):
                for j in range(8):
                    low(OUT0 + 8 * n + j, j)
                    if n and j == 3:
                        residual(n - 1)
            residual(3)
            dve.wait_ge(s("a2"), 1)
            dve.wait_ge(s("rms2"), 1)
            own.did(dve.reciprocal(RSTD[:, :], RSTD[:, :])); own.wait()
            dve.wait_ge(s("xm_new"), 4)

            def h2_low(q):
                split_low("h2_hi", q + 1, HX[:, 2 * q:2 * q + 2, 1, :], flat(MG[:, q // 2, q % 2 * 512:q % 2 * 512 + 512]),
                          HX[:, 2 * q:2 * q + 2, 0, :], "h2_lo")

            dve.wait_ge(used, OUT0 + 32 + 4)
            for q in range(8):
                b = MG[:, q // 2, q % 2 * 512:q % 2 * 512 + 512]
                for t in range(2):
                    k = 2 * q + t
                    own.did(stt(b[:, t * T:t * T + T], XM[:, k, :], A2[:, k:k + 1], RSTD[:, :], ALU.mult, ALU.mult))
                own.wait()
                for t in range(2):
                    k = 2 * q + t
                    i = ts(b[:, t * T:t * T + T], b[:, t * T:t * T + T], MC2[:, KT + k:KT + k + 1], None, ALU.add)
                i.then_inc(s("h2_float"), 1)
                if q:
                    h2_low(q - 1)
            h2_low(7)
            for n in range(4):
                dve.memset(ACC[:, n, :], 0.0).then_inc(s("down_read"), 1)

            def ffn_gated(m, last):
                dve.wait_ge(s("ffn_sig"), m + 1)
                tt(flat(TG), pair(0), flat(SG), ALU.mult).then_inc(s("ffn_gate_read"), 1)

            def hidden(m, last):
                dve.wait_ge(used, last + 1 + 4)
                dve.wait_ge(s("ffn_gate_read"), m + 1)
                tt(flat(HD), pair(2), flat(TG), ALU.mult).then_inc(s("hid_float"), 1)

            def hidden_low(m):
                dve.wait_ge(s("hid_hi"), m + 1)
                tt(HID[:, :, 1, :], HD.rearrange("p (k t) -> p k t", k=4), HID[:, :, 0, :], ALU.subtract).then_inc(s("hid_lo"), 1)

            def down(m, n, last):
                dve.wait_ge(used, last + 1 + 4)
                dve.wait_ge(s("down_read"), m * 4 + (n + 1))
                tt(flat(ACC[:, n, :]), pair(4 + 2 * (n % 2)), flat(ACC[:, n, :]), ALU.add).then_inc(s("down_read"), 1)

            for w in range(16):
                low(FFN0 + w, w)
                if w == 12:
                    ffn_gated(0, None)

            def chunk(m, mod):
                base = LOOP0 - 24 + m * 24
                for w in range(24):
                    low(base + w, w)
                    if mod and w % 3 == 2:
                        j = w // 3
                        mod_piece(None, j, m * 64 + (12 - 1) * 64 + 16 * (j // 2 + 1),
                                  ACCG[:, bass.ds(m - 1, 1), :].rearrange("p o n -> p (o n)"), False)
                    if w == 3:
                        hidden(m - 1, base - 1)
                    if w == 5:
                        hidden_low(m - 1)
                    if w == 12:
                        ffn_gated(m, None)
                    if w in (13, 15, 17, 19):
                        n = (w - 13) // 2
                        down(m - 1, n, base + 9 + 2 * n)

            with dve.Fori(1, 5) as m:
                own.enter(m, 1, 16)
                chunk(m, True)
                own.leave(1, 4)
            own.wait()
            dve.memset(ST[:, 60:61], 0.0).then_inc(s("accg_made"), 1)
            with dve.Fori(5, FC) as m:
                chunk(m, False)
            for w in range(8):
                low(LAST0 + w, w)
                if w == 3:
                    hidden(FC - 1, LAST0 - 1)
                    hidden_low(FC - 1)
            dve.wait_ge(s("gate2_summed"), 1)
            own.did(tt(MC2[:, 3 * KT:4 * KT], ps[:, 0, 0:KT], PA[:, 80:96], ALU.add))
            own.wait()
            for n in range(4):
                down(FC - 1, n, LAST0 + 2 * n + 1)
                dve.wait_ge(s("down_read"), 4 * FC + n + 1)
                for k in range(4):
                    kk = 4 * n + k
                    i = stt(XM[:, kk, :], ACC[:, n, k * T:k * T + T], MC2[:, 3 * KT + kk:3 * KT + kk + 1], XM[:, kk, :],
                            ALU.mult, ALU.add)
                i.then_inc(s("xf_new"), 1)
            dve.wait_ge(s("rms3"), 1)
            own.did(dve.reciprocal(RSTD[:, :], RSTD[:, :])); own.wait()
            dve.wait_ge(s("sqf"), 4)
            dve.wait_ge(s("xf_new"), 4)
            for k in range(KT):
                stt(XM[:, k, :], XM[:, k, :], PB[:, PB_GF + k:PB_GF + k + 1], RSTD[:, :], ALU.mult, ALU.mult).then_inc(s("y"), 1)

        @block.tensor
        def _(pe):
            mm = pe.matmul

            def turn(o, src, start=True):
                n = src.shape[0]
                return mm(o, src, IDENT[0:n, 0:n], start=start, stop=True, is_transpose=True, skip_group_check=True)

            def rows3(o, wh, wl, xh, xl, first, last):
                mm(o, wh, xh, start=first, stop=False, skip_group_check=True)
                mm(o, wh, xl, start=False, stop=False, skip_group_check=True)
                return mm(o, wl, xh, start=False, stop=last, skip_group_check=True)

            def ready(p):
                pe.wait_ge(lo_done, p + 1 + 4)

            def weights(j, t, f):
                a = slice(t * BW + f * P, t * BW + f * P + P)
                return HI[:, j % RING, a], LO[:, j % RING, a]

            def piece(p, j, moving, outs, k0, first, last):
                ready(p)
                for t in range(2):
                    xh, xl = moving(k0 + t)
                    for f in range(4):
                        o, opens = outs(f)
                        i = rows3(o, *weights(j, t, f), xh, xl, first and t == 0 and opens, last and t == 1)
                i.then_inc(used, 1)

            def piece_rows(p, j, lhs, outs, k0, first, last):
                ready(p)
                for t in range(2):
                    wh, wl = HI[:, j % RING, t * BW:(t + 1) * BW], LO[:, j % RING, t * BW:(t + 1) * BW]
                    for q, o in enumerate(outs):
                        xh, xl = lhs(k0 + t, q)
                        mm(o, xh, wh, start=first and t == 0, stop=False, skip_group_check=True)
                        mm(o, xh, wl, start=False, stop=False, skip_group_check=True)
                        i = mm(o, xl, wh, start=False, stop=last and t == 1, skip_group_check=True)
                i.then_inc(used, 1)

            def halves(b):
                return lambda f: (ps[:, b + f // 2, f % 2 * T:f % 2 * T + T], f % 2 == 0)

            def banks(b):
                return lambda f: (ps[:, b + f, :], True)

            def both(k):
                return H[:, :, k, 0, :], H[:, :, k, 1, :]

            def only_x(k):
                return HX[:, k, 0, :], HX[:, k, 1, :]

            def turned_tokens(k, q):
                a = slice(q % 2 * P, q % 2 * P + P)
                return H[:, q // 2, k, 0, a], H[:, q // 2, k, 1, a]

            pe.wait_ge(s("cst_in"), 16)
            pe.wait_ge(s("rows_in"), 16 * 12)
            turn(ps[:, 6, 0:P], PAROW).then_inc(used, 1)
            turn(ps[:, 7, 0:PB_N], PBROW).then_inc(used, 1)
            turn(ps[:, 0, 0:P], PAROW).then_inc(used, 1)
            turn(ps[:, 1, 0:P], PAROW).then_inc(used, 1)
            turn(ps[:, 2, 0:P], PAROW).then_inc(s("params_turned"), 1)
            for b in range(16):
                pe.wait_ge(s("rows_scaled"), b // 4 + 1)
                if b in (6, 7):
                    pe.wait_ge(s("params"), 1)
                if b >= 8:
                    pe.wait_ge(s("xt_dve" if b % 2 else "xt_act"), (b - 8) // 2 + 1)
                for k in range(4):
                    kk = b % 4 * 4 + k
                    i = turn(ps[:, b % 8, k * P:k * P + P], XTOK[:, b // 4, kk * P:kk * P + P], start=k == 0)
                i.then_inc(s("x_turned"), 1)
            pe.wait_ge(s("sc_lo"), 1)
            pe.wait_ge(s("xt_dve"), 8)
            pe.wait_ge(s("xt_act"), 8)
            for n in range(8):
                o = ps[0:4, n, :]
                for j in range(8):
                    ready(n * 8 + j)
                    for t in range(2):
                        for w, part in enumerate((HI, LO)):
                            i = mm(o, SC[:, 2 * j + t, :], part[:, j % RING, t * BW:(t + 1) * BW],
                                   start=j + t + w == 0, stop=j + t + w == 9, skip_group_check=True)
                    i.then_inc(used, 1)
            pe.wait_ge(s("mrow"), 1)
            for j in range(32):
                i = mm(ps[:, 7, 2 * j:2 * j + 2], MROW[:, j * P:(j + 1) * P], CST[0:4, CST_SEL:CST_SEL + 2],
                       start=j == 0, stop=True, skip_group_check=True)
            i.then_inc(s("mod1_turned"), 1)

            def straight(w):
                if w == 18:
                    pe.wait_ge(s("small_in"), 16 * 7)
                    for g in range(G4):
                        i = turn(ps[:, 2, g * P:g * P + P], SW[:, 4 + g, :], start=g == 0)
                    i.then_inc(s("wsp_turned"), 1)
                for half, w0 in enumerate((ATT_A, ATT_B)):
                    if w == w0:
                        pe.wait_ge(s("win_read"), 4)
                        pe.wait_ge(s("tb"), 1)
                        if half:
                            pe.wait_ge(s("att_out"), 2)
                            pe.wait_ge(s("pt"), 4)
                        for u in range(4):
                            h, t = 2 * half + u // 2, u % 2
                            o = ps[:, 4 + u, :]
                            mm(o, QT[:, h, t * P:t * P + P], KTT[:, h, :], start=True, stop=False, skip_group_check=True)
                            mm(o[:, T:2 * T], IDENT, TB[:, h, 2 - 2 * t:6 - 2 * t, :], start=False, stop=True,
                               skip_group_check=True).then_inc(s("scores"), 1)
                    if w == w0 + 7:
                        for u in range(4):
                            pe.wait_ge(s("probs"), 4 * half + u + 1)
                            for j in range(4):
                                i = turn(ps[:, 4 + u, j * P:j * P + P], PR[:, u, j * P:j * P + P], start=j == 0)
                            i.then_inc(s("p_turned"), 1)
                    if w == w0 + 12:
                        for hh in range(2):
                            h = 2 * half + hh
                            pe.wait_ge(s("pt"), 4 * half + 2 * hh + 2)
                            for j in range(4):
                                i = mm(ps[:, 4 + 2 * hh, 0:T], VAL[:, j, h * P:h * P + P], PT[:, hh, j, :], start=j == 0,
                                       stop=j == 3, skip_group_check=True)
                            i.then_inc(s("att_av"), 1)
                if w == 72:
                    pe.wait_ge(s("att_out"), 4)
                    pe.wait_ge(s("pooled"), 1)
                    for g in range(G4):
                        i = mm(ps[:, 4 + g // 2, g % 2 * T:g % 2 * T + T], SW[:, g, :], YF[:, g, :], start=g % 2 == 0,
                               stop=True, skip_group_check=True)
                    i.then_inc(s("pool_mm"), 1)
                    pe.wait_ge(s("vn"), 2)
                    pe.wait_ge(s("wspt"), 1)
                    for t in range(2):
                        for g in range(G4):
                            i = mm(ps[:, 6 + t, g * P:g * P + P], V[:, t, g * P:g * P + P], WSPT[:, g, :], start=g == 0,
                                   stop=True, skip_group_check=True)
                    i.then_inc(s("sgu_mm"), 1)
                for g in range(G4):
                    if w == LRU_0 + LRU_STEP * g:
                        pe.wait_ge(s("conv"), g + 1)
                        pe.wait_ge(s("pool_lo"), 4)
                        pe.wait_ge(s("sgu_float"), 1)
                        if g:
                            pe.wait_ge(s("lru_i"), 2 * g)
                        for d in range(2):
                            mm(ps[:, 4 + 2 * d, :], SW[:, 8 + 4 * d + g, :], Z[:, g % 2, :], start=True, stop=True)
                            mm(ps[:, 5 + 2 * d, :], SW[:, 16 + 4 * d + g, :], Z[:, g % 2, :], start=True, stop=True)\
                                .then_inc(s("lru_mm"), 1)

            win_wait = {2: 1, 3: 2, 4: 3, 5: 1, 6: 5, 7: 6}
            for n, sl in enumerate(WIN_ORDER):
                if n in win_wait:
                    pe.wait_ge(s("win_read"), win_wait[n])
                if n == 5:
                    pe.wait_ge(s("wspt"), 1)
                for j in range(8):
                    p = WIN0 + 8 * n + j
                    if n == 0:
                        pe.wait_ge(s("h_lo"), j + 1)
                    k0, first, last = 2 * j, j == 0, j == 7
                    if sl in (S_K, S_LRU):
                        piece(p, j, both, banks(0 if sl == S_K else 4), k0, first, last)
                    elif sl == S_VAL:
                        piece_rows(p, j, turned_tokens, [ps[:, 4 + q, :] for q in range(4)], k0, first, last)
                    elif sl == S_V:
                        piece_rows(p, j, lambda k, q: turned_tokens(k, 2 + q), [ps[:, 2 + q, :] for q in range(2)], k0, first, last)
                    else:
                        piece(p, j, only_x, halves(2 if sl == S_LG else 0), k0, first, last)
                    straight(8 * n + j)
                    if sl == S_LRU and j == 7:
                        mm(ps[:, 3, 0:2], IDENT, CST[:, 0:2], start=True, stop=True, skip_group_check=True).then_inc(s("h_last_read"), 1)

            def gate_group(base, n):
                for j in range(8):
                    piece(base + 8 * n + j, j, only_x, halves(2 * (n % 2)), 2 * j, j == 0, j == 7)
                    yield 8 * n + j

            def branch_group(base, n):
                for j in range(2):
                    piece(base + 32 + 2 * n + j, 2 * n + j, lambda k: (Y[:, k, 0, :], Y[:, k, 1, :]), halves(2 * (n % 2)),
                          4 * n + 2 * j, j == 0, j == 1)

            for n in range(NB):
                if n < 2:
                    pe.wait_ge(s("win_read"), 7 + n)
                else:
                    pe.wait_ge(s("gate_read"), n - 1)
                for w in gate_group(MIX0, n):
                    straight(64 + w)
            y_ready = ("pool_lo", "sgu_lo", "lru_lo", "att_out")
            for n in range(NB):
                pe.wait_ge(s(y_ready[n]), 1 if n == 1 else 4)
                if n < 2:
                    pe.wait_ge(s("gate_read"), 3 + n)
                else:
                    pe.wait_ge(s("merge_read"), n - 1)
                branch_group(MIX0, n)

            def mod_sum(n):
                for k in range(4):
                    i = mm(ps[:, 4 + n % 2, k:k + 1], ACCM[:, n % 2, k * P:(k + 1) * P], ONES[:, 0:1], start=k == 0, stop=True,
                           skip_group_check=True)
                i.then_inc(s("mod_summed"), 1)

            with pe.Fori(1, 4) as f:
                base = MIX0 + f * BLK
                for n in range(NB):
                    if n < 2:
                        pe.wait_ge(s("merge_read"), f * 4 + (n - 1))
                    else:
                        pe.wait_ge(s("gate_read"), f * 4 + (n - 1))
                    for w in gate_group(base, n):
                        if n and w % 8 == 1:
                            pe.wait_ge(s("acc_made"), f * 4 + (n - 4))
                            mod_sum(n - 1)
                for n in range(NB):
                    if n < 2:
                        pe.wait_ge(s("gate_read"), f * 4 + (3 + n))
                    else:
                        pe.wait_ge(s("merge_read"), f * 4 + (n - 1))
                    branch_group(base, n)
                    if n == 0:
                        pe.wait_ge(s("acc_made"), f * 4)
                        mod_sum(3)

            pe.wait_ge(s("x_again"), 32)
            for b in range(8):
                if b >= 4:
                    pe.wait_ge(s("xm_set"), b - 3)
                for k in range(4):
                    kk = b % 4 * 4 + k
                    i = turn(ps[:, 4 + b % 4, k * P:k * P + P], XT2[:, b // 4, kk * P:kk * P + P], start=k == 0)
                i.then_inc(s("x_turned_again"), 1)

            def sum_squares(n, name, count, first, last):
                pe.wait_ge(s(name), count)
                for k in range(4):
                    i = mm(ps[:, 6, 0:T], ONES[:, :], SQ[:, k * T:k * T + T], start=first and k == 0, stop=last and k == 3,
                           skip_group_check=True)
                i.then_inc(s("sq_used"), 1)

            for n in range(4):
                if n < 2:
                    pe.wait_ge(s("merge_read"), 15 + n)
                else:
                    pe.wait_ge(s("xm_new"), n - 1)
                for j in range(8):
                    if n == 0 and j % 2 == 0:
                        pe.wait_ge(s("mg_lo"), j // 2 + 1)
                    if n == 0 and j == 0:
                        pe.wait_ge(s("xm_set"), 8)
                    piece(OUT0 + 8 * n + j, j, only_x, halves(2 * (n % 2)), 2 * j, j == 0, j == 7)
                    if n and j == 7:
                        sum_squares(n - 1, "sq", n, n == 1, False)
            sum_squares(3, "sq", 4, False, True)

            for w in range(16):
                if w < 8:
                    pe.wait_ge(s("h2_lo"), w + 1)
                if w == 0:
                    pe.wait_ge(s("xm_new"), 4)
                piece(FFN0 + w, w, only_x, halves(2 * (w // 8)), w % 8 * 2, w % 8 == 0, w % 8 == 7)

            def down_group(base, n):
                for j in range(2):
                    piece(base + 2 * n + j, 2 * n + j, lambda k: (HID[:, k, 0, :], HID[:, k, 1, :]), halves(4 + 2 * (n % 2)),
                          2 * j, j == 0, j == 1)

            with pe.Fori(1, FC) as m:
                base = LOOP0 - 24 + m * 24
                pe.wait_ge(s("ffn_gate_read"), m)
                for j in range(8):
                    piece(base + j, j, only_x, halves(0), 2 * j, j == 0, j == 7)
                pe.wait_ge(s("hid_lo"), m)
                for n in range(4):
                    pe.wait_ge(s("down_read"), m * 4 + (n - 1))
                    down_group(base + 8, n)
                pe.wait_ge(s("hid_float"), m)
                for j in range(8):
                    piece(base + 16 + j, j, only_x, halves(2), 2 * j, j == 0, j == 7)
            pe.wait_ge(s("accg_made"), 1)
            pe.wait_ge(s("ffn_gate_read"), FC)
            for k in range(KT):
                i = mm(ps[:, 0, k:k + 1], ACCG[:, k // 4, k % 4 * P:k % 4 * P + P], ONES[:, 0:1], start=k == 0, stop=True,
                       skip_group_check=True)
            i.then_inc(s("gate2_summed"), 1)
            pe.wait_ge(s("hid_lo"), FC)
            for n in range(4):
                pe.wait_ge(s("down_read"), FC * 4 + (n - 1))
                down_group(LAST0, n)
            for n in range(4):
                if n == 0:
                    pe.wait_ge(s("down_read"), 4 * FC + 4)
                sum_squares(n, "sqf", n + 1, n == 0, n == 3)
            for b in range(8):
                t, n = b // 4, b % 4
                if b == 0:
                    pe.wait_ge(s("xf_new"), 1)
                if b >= 4:
                    pe.wait_ge(s("out_rows"), b - 3)
                pe.wait_ge(s("y"), 4 * n + 4)
                for k in range(4):
                    i = turn(ps[:, n, k * P:k * P + P], XM[:, 4 * n + k, t * P:t * P + P], start=k == 0)
                i.then_inc(s("y_turned"), 1)


_INS = ['x', 'c', 'ctx', 'c_ctx', 'w_mod', 'b_mod', 'g_mix', 'g_ffn', 'g_final', 'w_in', 'w_pool', 'pool_scale',
        'gmlp_ln_g', 'w_sp', 'b_sp', 'conv_w', 'conv_b', 'w_rg', 'b_rg', 'w_ig', 'b_ig', 'lru_lam', 'rpb',
        'w_branch', 'w_gate', 'w_out', 'w_ffn_gate', 'w_ffn_up', 'w_ffn_down']


def shape_constants():
    cst = np.zeros((P, CST_N), np.float32)
    cst[:, 0:P] = np.eye(P)
    col = np.arange(GRID)
    start = np.clip(col - WIN_C // 2, 0, GRID - WIN_C)
    ok = (col[None, :] >= start[:, None]) & (col[None, :] < start[:, None] + WIN_C)
    cst[:, CST_MASK:CST_MASK + GRID] = np.tile(np.where(ok, 0.0, MASKED), (2, 1))
    cst[0:4, CST_SEL:CST_SEL + 2] = [[1, 0], [0, 1], [1, 0], [0, 1]]
    t = np.arange(T)
    rc = [1.0 / (np.clip(t + w // 2, 0, T) - np.clip(t - w // 2, 0, T)) for w in POOL_WINDOWS]
    return cst, np.concatenate(rc).astype(np.float32)


def kernel(**inputs):
    import concourse.bacc as _bacc
    from concourse.bass_utils import run_bass_kernel_spmd as _run

    nc = _bacc.Bacc("TRN2", target_bir_lowering=False, num_devices=1)
    arrays, args = {}, []
    cst, rc = shape_constants()
    for name, a in [(n, inputs[n]) for n in _INS] + [("cst", cst), ("rc", rc)]:
        a = np.ascontiguousarray(a)
        arrays[f"in_{name}"] = a
        args.append(nc.dram_tensor(f"in_{name}", a.shape, mybir.dt.from_np(a.dtype), kind="ExternalInput").ap())
    args.append(nc.dram_tensor("out_0", (1, T, D), F32, kind="ExternalOutput").ap())
    build(nc, *args)
    r = _run(nc, [arrays], core_ids=[0])
    return r.results[0]["out_0"]
```

```python
from contextlib import ExitStack

import numpy as np

import concourse.bass as bass
from concourse import mybir

F32 = mybir.dt.float32
F32R = mybir.dt.float32r
ALU = mybir.AluOpType
ACT = mybir.ActivationFunctionType
AX_X = mybir.AxisListType.X

P = 128
D = 2048
T = 256
KT = D // P
BW = 512
G4 = BW // P
NB = 4
DFF = 5632
FC = DFF // BW
RING = 4
PC = 2 * BW
GRID = 64
WIN_R, WIN_C = 8, 16
POOL_WINDOWS = (2, 4, 8, 16)
PAD = 8
ZW = T + 2 * PAD
CONV = 4
LW = T + CONV
EPS = 1e-6
MASKED = -1e30
NDR = 7
PITCH = 128

START = [("mod", q, j) for q in range(2) for j in range(16)]
for _i in range(4):
    START += [("keys", _i // 2, _i % 2)] + [("mod", 2 + _i // 2, _i % 2 * 8 + j) for j in range(8)]
START += [("keys", q, j) for q in (2, 3) for j in range(2)]
STARTED = len(START)
START_RING = 8
WHOLE = {p for p, (kind, q, j) in enumerate(START) if kind == "mod" and q < 2 and j % 8 in (2, 4, 6)}
MOD_TURN = [23, START.index(("mod", 1, 15)) + 4, START.index(("mod", 2, 15)) + 4, STARTED - 4]


def after_turn(q, steps):
    return STARTED - 1 if q == 3 else MOD_TURN[q] + 3 + steps


WIN0 = STARTED - 8
MIX0 = WIN0 + 8 * 8
BLK = NB * 8 + NB * 2
OUT0 = MIX0 + 4 * BLK
FFN0 = OUT0 + 4 * 8
LOOP0 = FFN0 + 16
PRE0 = LOOP0 + (FC - 2) * 24
LAST0 = PRE0 + 24

S_POOL, S_U, S_V, S_LRU, S_LG, S_Q, S_K, S_VAL = range(8)
WIN_ORDER = (S_K, S_VAL, S_Q, S_LRU, S_POOL, S_V, S_U, S_LG)

PA_BMOD, PA_GMIX, PA_GFFN = 0, 96, 112
PB_PS, PB_CW, PB_CB, PB_BR, PB_BI, PB_LAM = 0, 4, 20, 24, 32, 40
PB_N = 48
CST_MASK, CST_N = 128, 192

ATT_A, ATT_B = 32, 49
POOL_AT = (58, 60, 62, 64)
SMALL_MM = 67
MOD2_0, EARLY, MOD_TILES = 24, 3, 3 * KT
MOD_AT = [[t for t in range(MOD_TILES) if 2 + t * (BLK - 2) // MOD_TILES == w] for w in range(BLK)]
LRU_AT = (71, 77, 83, 88)


class Own:

    def __init__(self, eng, sem):
        self.eng, self.sem, self.n, self.i, self.per = eng, sem, 0, None, 0

    def did(self, ins):
        ins.then_inc(self.sem, 1)
        self.n += 1
        return ins

    def wait(self, back=0):
        n = self.n - back
        self.eng.wait_ge(self.sem, n if self.i is None else n + self.i * self.per)

    def enter(self, i, first, per):
        self.i, self.per, self.n0 = i, per, self.n
        self.n -= first * per

    def leave(self, first, count):
        assert self.n + first * self.per - self.n0 == self.per, (self.n + first * self.per - self.n0, self.per)
        self.i = None
        self.n = self.n0 + count * self.per


def build(nc, x, c, ctx, c_ctx, w_mod, b_mod, g_mix, g_ffn, g_final, w_in, w_pool, pool_scale,
          gmlp_ln_g, w_sp, b_sp, conv_w, conv_b, w_rg, b_rg, w_ig, b_ig, lru_lam, rpb,
          w_branch, w_gate, w_out, w_ffn_gate, w_ffn_up, w_ffn_down, cst, rc, out):
    ctxs = ExitStack()
    with ctxs:
        def sb(name, shape, dt=F32):
            return ctxs.enter_context(nc.sbuf_tensor(name, shape, dt))

        def sem(name):
            return ctxs.enter_context(nc.semaphore(name))

        RAW = sb("RAW", [P, RING, PC])
        HI = sb("HI", [P, RING, PC], F32R)
        LO = sb("LO", [P, RING, PC], F32R)
        H = sb("H", [P, 2, KT, 2, T], F32R)
        HX = H[:, 1, :, :, :]
        Y = H[:, 0, :, :, :]
        HID = H[:, 0, 0:G4, :, :]
        HIDL = H[:, 0, G4:2 * G4, :, :]
        SC = sb("SC", [P, KT, 4], F32R)
        SCF = sb("SCF", [P, 2, KT])
        CST = sb("CST", [P, CST_N])
        IDENT = CST[:, 0:P]
        PA = sb("PA", [P, P])
        PB = sb("PB", [P, PB_N])
        MC1 = sb("MC1", [P, 2 * KT, 2])
        A1 = sb("A1", [P, KT, 2])
        MC2 = sb("MC2", [P, 4 * KT])
        A2 = sb("A2", [P, KT])
        EPSC = sb("EPSC", [P, 1])
        ST = sb("ST", [P, 64])
        LRC = sb("LRC", [P, 8, 8])
        MR = sb("MR", [P, 2, BW])
        ACCM = sb("ACCM", [P, 2, BW])
        RSTD = ACCM[:, 0, 0:T]

        ATT = sb("ATT", [P, 8704])
        XT = ATT[:, 0:8192].rearrange("p (s k t) -> p s k t", s=2, k=KT)
        PAROW = ATT[:, 8192:8320]
        PBROW = ATT[0:PB_N, 8320:8448]
        RP = ATT[0:NB * NDR, 8448:8576]
        KTT = ATT[:, 0:2048].rearrange("p (h t) -> p h t", h=G4)
        VAL = ATT[:, 2048:4096].rearrange("p (s n) -> p s n", s=4)
        QT = ATT[:, 4096:5120].rearrange("p (h t) -> p h t", h=G4)
        TB = ATT[:, 5120:6656].rearrange("p (h j n) -> p h j n", h=G4, j=6)
        PT = ATT[:, 6656:8704].rearrange("p (h j t) -> p h j t", h=2, j=4)
        S4 = ATT[:, 0:4096].rearrange("p (n e) -> p n e", n=NB)
        MG = ATT[:, 4096:8192].rearrange("p (f e) -> p f e", f=4)
        LT = ATT[:, 4096:8192].rearrange("p (u a e) -> p u a e", u=2, a=4)
        ACC = ATT[:, 0:4096].rearrange("p (n e) -> p n e", n=4)
        SG = ATT[:, 4096:5120]
        TG = ATT[:, 5120:6144]
        HD = ATT[:, 6144:7168]

        BR = sb("BR", [P, 12896])
        XTOK = BR[:, 0:8192].rearrange("p (s n) -> p s n", s=4)
        MROW = BR[0:4, 8192:9216]
        RAWX = BR[:, 10240:12288].rearrange("p (s e) -> p s e", s=2)
        CROW = BR[0:2 * KT, 12288:12416]
        LP = BR[:, 0:2080].rearrange("p (g s w) -> p g s w", g=G4, s=2)
        LG = BR[:, 2080:3104]
        RC = BR[:, 2080:3104].rearrange("p (g t) -> p g t", g=G4)
        U = BR[:, 3104:4128].rearrange("p (g t) -> p g t", g=G4)
        V = BR[:, 4128:5152].rearrange("p (s n) -> p s n", s=2)
        ZP = BR[:, 5152:6240].rearrange("p (g w) -> p g w", g=G4)
        Z = BR[:, 6240:7264].rearrange("p (b e) -> p b e", b=2)
        YF = BR[:, 7264:8288].rearrange("p (g t) -> p g t", g=G4)
        PR = BR[:, 6240:8288].rearrange("p (u e) -> p u e", u=4)
        SW = BR[:, 8288:11360].rearrange("p (m n) -> p m n", m=24)
        WSPT = BR[:, 11360:11872].rearrange("p (g n) -> p g n", g=G4)
        LNG = BR[:, 11872:12384]
        BSP = BR[:, 12384:12896]
        HS = BR[:, 11360:11616]
        XT2 = BR[:, 0:4096].rearrange("p (s n) -> p s n", s=2)
        ACCG = BR[:, 0:2048].rearrange("p (m n) -> p m n", m=4)
        XM = BR[:, 4096:8192].rearrange("p (k t) -> p k t", k=KT)
        MR4 = BR[:, 8192:10240].rearrange("p (s e) -> p s e", s=4)
        ACCB = BR[:, 10368:11904].rearrange("p (s e) -> p s e", s=3)
        SQ = BR[:, 2048:3072]
        GFB = BR[:, 10368:12416]
        ONES = BR[:, 10240:10240 + P]
        OTOK = ATT[:, 4096:8192].rearrange("p (s n) -> p s n", s=2)

        ps = ctxs.enter_context(nc.psum_tensor("ps", [P, 8, BW], F32))

        def pair(b):
            return ps[:, b:b + 2, :]

        def raw_first(p):
            r = p % START_RING
            extra = (RAWX[:, 0, :], RAWX[:, 1, :], MR.rearrange("p s e -> p (s e)"), ACCM.rearrange("p s e -> p (s e)"))
            return RAW[:, r, :] if r < RING else extra[r - RING]

        def flat(ap):
            return ap.rearrange("p (b e) -> p b e", b=2)

        toeplitz = nc.dram_tensor("toeplitz_rows", [NB * NDR * GRID * PITCH], F32, kind="Internal").ap()

        landed = [sem(f"piece_landed{s}") for s in range(RING)]
        landed_first = [sem(f"first_landed{s}") for s in range(START_RING)]
        hi_done = sem("hi_done")
        lo_done = sem("lo_done")
        used = sem("piece_used")
        own_a, own_v = sem("act_own"), sem("dve_own")
        S = {}

        def s(name):
            if name not in S:
                S[name] = sem(name)
            return S[name]

        def view(w):
            return w.rearrange("(q t p) n -> p q t n", t=2, p=P)

        v_mod, v_in, v_out = view(w_mod[0]), view(w_in[0]), view(w_out[0])
        v_gate = w_gate[0].rearrange("(q t p) b n -> p q t (b n)", t=2, p=P)
        v_branch = w_branch[0].rearrange("b (q t p) n -> p (b q) t n", t=2, p=P)
        v_fg, v_fu, v_fd = view(w_ffn_gate[0]), view(w_ffn_up[0]), view(w_ffn_down[0])

        block = ctxs.enter_context(nc.Block())

        @block.sync
        def _(sp):
            def first_piece(p, view, q, col):
                last = p - START_RING
                if last in WHOLE:
                    sp.wait_ge(used, last + 1 + 4)
                elif last >= 0:
                    sp.wait_ge(lo_done, last + 1 + 4)
                sp.dma_start(raw_first(p).rearrange("p (t n) -> p t n", t=2),
                             view[:, q, :, col:col + BW]).then_inc(landed_first[p % START_RING], 16)

            def piece(p, j, view, q, col):
                sp.wait_ge(lo_done, p + 1)
                sp.dma_start(RAW[:, j % RING, :].rearrange("p (t n) -> p t n", t=2),
                             view[:, q, :, bass.ds(col, BW)]).then_inc(landed[j % RING], 16)

            sp.dma_start(CROW[0:KT, :], c[0].rearrange("(a n) -> a n", n=P)).then_inc(s("crow_in"), 16)
            sp.dma_start(CROW[KT:2 * KT, :], c_ctx.rearrange("(a n) -> a n", n=P)).then_inc(s("crow_in"), 16)
            sp.dma_start(CST[:, :], cst).then_inc(s("cst_in"), 16)
            tokens = (ctx[0, 0:P, :], ctx[0, P:T, :], x[0, 0:P, :], x[0, P:T, :])
            for p, (kind, q, j) in enumerate(START):
                if kind == "mod":
                    first_piece(p, v_mod, j % 8, j // 8 * D + q * BW)
                else:
                    first_piece(p, v_in, 2 * q + j, S_K * BW)
                if p in (3, 5, 7, 9):
                    k = (p - 3) // 2
                    sp.dma_start(XTOK[:, k, :], tokens[k]).then_inc(s(f"tokens{k}"), 16)
            for n, sl in enumerate(WIN_ORDER):
                if n == 0:
                    continue
                for j in range(8):
                    piece(WIN0 + 8 * n + j, j, v_in, j, sl * BW)

            def gates(f, base):
                with sp.Fori(0, NB) as n:
                    for j in range(8):
                        piece(base + n * 8 + j, j, v_gate, j, n * D + f * BW)

            def branches(f, base):
                for j in range(8):
                    piece(base + 32 + j, j, v_branch, j, f * BW)

            with sp.Fori(0, 4) as f:
                gates(f, MIX0 + f * BLK)
                branches(f, MIX0 + f * BLK)
            with sp.Fori(0, 4) as n:
                for j in range(8):
                    piece(OUT0 + n * 8 + j, j, v_out, j, n * BW)
            for j in range(8):
                piece(FFN0 + j, j, v_fg, j, 0)
            for j in range(8):
                piece(FFN0 + 8 + j, j, v_fu, j, 0)
            with sp.Fori(1, FC - 1) as m:
                base = LOOP0 - 24 + m * 24
                for j in range(8):
                    piece(base + j, j, v_fg, j, m * BW)
                for j in range(8):
                    sp.wait_ge(lo_done, base + 8 + j + 1)
                    sp.dma_start(RAW[:, j % RING, :].rearrange("p (t n) -> p t n", t=2),
                                 v_fd[:, bass.ds(m * 2 - 2 + j % 2, 1), :, j // 2 * BW:j // 2 * BW + BW])\
                        .then_inc(landed[j % RING], 16)
                for j in range(8):
                    piece(base + 16 + j, j, v_fu, j, m * BW)
            for j in range(8):
                piece(PRE0 + j, j, v_fg, j, (FC - 1) * BW)
            for j in range(8):
                piece(PRE0 + 8 + j, j, v_fu, j, (FC - 1) * BW)
            for j in range(8):
                piece(PRE0 + 16 + j, j, v_fd, 2 * FC - 4 + j % 2, j // 2 * BW)
            for j in range(8):
                piece(LAST0 + j, j, v_fd, 2 * FC - 2 + j % 2, j // 2 * BW)
            for half in range(2):
                for t in range(2):
                    sp.wait_ge(s(f"rows_done{t}"), half + 1)
                    cols = slice(half * D // 2, (half + 1) * D // 2)
                    sp.dma_start(out[0, t * P:(t + 1) * P, cols], OTOK[:, t, cols]).then_inc(s(f"stored{t}"), 16)
            for t in range(2):
                sp.wait_ge(s(f"stored{t}"), 32)

        @block.gpsimd
        def _(pool):
            rows = [(PAROW, 0, b_mod[0].rearrange("(a n) -> a n", n=P)),
                    (PAROW, PA_GMIX, g_mix[0].rearrange("(a n) -> a n", n=P)),
                    (PAROW, PA_GFFN, g_ffn[0].rearrange("(a n) -> a n", n=P)),
                    (PBROW, PB_PS, pool_scale[0].rearrange("(a n) -> a n", n=P)),
                    (PBROW, PB_CW, conv_w[0].rearrange("k (a n) -> (k a) n", n=P)),
                    (PBROW, PB_CB, conv_b[0].rearrange("(a n) -> a n", n=P)),
                    (PBROW, PB_BR, b_rg[0].rearrange("k (a n) -> (k a) n", n=P)),
                    (PBROW, PB_BI, b_ig[0].rearrange("k (a n) -> (k a) n", n=P)),
                    (PBROW, PB_LAM, lru_lam[0].rearrange("k (a n) -> (k a) n", n=P)),
]
            for dst, r0, src in rows:
                n = src.shape[0]
                pool.dma_start(dst[r0:r0 + n, :], src).then_inc(s("rows_in"), 16)
            pool.wait_ge(s("rp_zero"), 1)
            for h in range(NB):
                pool.dma_start(RP[h * NDR:(h + 1) * NDR, 48:48 + 2 * WIN_C - 1],
                               rpb[0, h, WIN_R - 4:WIN_R - 4 + NDR, :]).then_inc(s("rp_in"), 16)
            pool.wait_ge(s("rp_in"), 16 * NB)
            pool.dma_start(toeplitz.rearrange("(r c m) -> r c m", r=NB * NDR, c=GRID),
                           RP.unsqueeze(1).to_broadcast([NB * NDR, GRID, PITCH])).then_inc(s("toeplitz_out"), 16)
            pool.wait_ge(s("h_free"), 1)
            for i, (m0, src) in enumerate(((0, w_pool[0]), (4, w_sp[0]), (8, w_rg[0].rearrange("a g p n -> (a g) p n")),
                                           (16, w_ig[0].rearrange("a g p n -> (a g) p n")))):
                n = src.shape[0]
                pool.dma_start(SW[:, m0:m0 + n, :], src.rearrange("m p n -> p m n")).then_inc(s("small_in"), 16)
            pool.dma_start(LNG, gmlp_ln_g.to_broadcast([P, BW])).then_inc(s("small_in"), 16)
            pool.dma_start(BSP, b_sp.rearrange("a g n -> a (g n)").to_broadcast([P, BW])).then_inc(s("small_in"), 16)
            pool.dma_start(RC.rearrange("p g t -> p (g t)"), rc.rearrange("(a n) -> a n", a=1).to_broadcast([P, 4 * T]))\
                .then_inc(s("small_in"), 16)
            pool.wait_ge(s("toeplitz_out"), 16)
            for half in range(2):
                for h in range(NB):
                    src = bass.AP(toeplitz.tensor, (h * NDR + 1 - half) * GRID * PITCH + GRID - 1,
                                  [[PITCH - 1, GRID], [GRID * PITCH, 6], [1, GRID]])
                    pool.dma_start(TB[half * GRID:(half + 1) * GRID, h, :, :], src).then_inc(s("tb_in"), 16)
            def mod_group(g, slots, ring, landed):
                for k in range(KT):
                    pool.wait_ge(s("mod_used"), g * KT + (k + 3 - ring))
                    pool.dma_start(slots[:, k % ring, :], w_mod[0, k * P:(k + 1) * P, bass.ds(2 * D + g * BW, BW)])\
                        .then_inc(s(f"{landed}{k % ring}"), 16)

            with pool.Fori(0, EARLY) as g:
                mod_group(g, MR, 2, "mod_landed")
            pool.wait_ge(s("branches_made"), 1)
            with pool.Fori(EARLY, 9) as g:
                mod_group(g, MR4, 4, "mod4_landed")
            for t in range(2):
                pool.dma_start(XT2[:, t, :], x[0, t * P:(t + 1) * P, :]).then_inc(s("x_again"), 16)
            with pool.Fori(9, 16) as g:
                mod_group(g, MR4, 4, "mod4_landed")
            pool.wait_ge(s("mod_read"), 12)
            pool.dma_start(GFB, g_final.rearrange("(a n) -> a n", a=1).to_broadcast([P, D])).then_inc(s("gfb_in"), 16)

        @block.scalar
        def _(act):
            own = Own(act, own_a)

            def first_high(p):
                act.wait_ge(landed_first[p % START_RING], 16 * (p // START_RING + 1))
                act.wait_ge(used, p + 1)
                act.activation(HI[:, p % RING, :], raw_first(p), ACT.Copy).then_inc(hi_done, 2 if p + 1 in WHOLE else 1)

            def high(base4, j):
                act.wait_ge(landed[j % RING], base4 * 16 + 16 * (j // 4 + 1 - STARTED // RING))
                act.wait_ge(used, base4 * 4 + j + 1)
                act.activation(HI[:, j % RING, :], RAW[:, j % RING, :], ACT.Copy).then_inc(hi_done, 1)

            act.wait_ge(s("consts_set"), 1)
            act.wait_ge(s("c_turned"), 1)
            act.activation(ST[:, 16:48], ps[:, 6, 0:2 * KT], ACT.Sigmoid).then_inc(s("sigc"), 1)
            act.wait_ge(s("siluc"), 1)
            act.activation(SC[:, :, 0:2], SCF[:, :, :].rearrange("p w k -> p k w"), ACT.Copy).then_inc(s("sc_hi"), 1)

            def input_context(q):
                act.wait_ge(s("mod1_ready"), q // 2 + 1)
                if q == 0:
                    act.wait_ge(s("xt_act"), 8)
                    act.wait_ge(s("xt_dve"), 8)
                for k in (2 * q, 2 * q + 1):
                    i = act.activation(XT[:, 0, k, :], XT[:, 0, k, :], ACT.Identity, scale=A1[:, k, 1:2], bias=MC1[:, k, 1:2])
                i.then_inc(s("hc_float"), 1)

            def input_high(q):
                act.wait_ge(s("hc_float"), q + 1)
                act.wait_ge(s("h_float"), q + 1)
                act.activation(H[:, :, 2 * q:2 * q + 2, 0, :], XT[:, :, 2 * q:2 * q + 2, :], ACT.Copy).then_inc(s("h_hi"), 1)

            def start(p):
                if p in (7, 9, 11, 13):
                    k = (p - 7) // 2
                    act.wait_ge(s(f"tokens{k}"), 16)
                    act.activation(ATT[:, k * D:(k + 1) * D], XTOK[:, k, :], ACT.Square, accum_out=ST[:, k:k + 1])\
                        .then_inc(s("ssq"), 1)
                if p == 13:
                    act.wait_ge(s("ssq"), 4)
                    act.activation(ST[:, 4:8], ST[:, 0:4], ACT.Sqrt, bias=EPSC[:, 0:1], scale=1.0 / D).then_inc(s("rms"), 1)
                if 20 <= p < 28:
                    b = 2 * (p - 20)
                    act.wait_ge(s("x_turned"), b + 1)
                    act.activation(XT[:, b // 8, b % 4 * 4:b % 4 * 4 + 4, b // 4 % 2 * P:b // 4 % 2 * P + P],
                                   ps[:, b % 4, :].rearrange("p (k t) -> p k t", k=4), ACT.Copy).then_inc(s("xt_act"), 1)
                for q in range(4):
                    for part in range(2):
                        done = START.index(("mod", q, 8 * part + 7))
                        if p == done + 4:
                            act.wait_ge(used, done + 1 + 4)
                            if q:
                                act.wait_ge(s("mod1_turned"), q)
                            act.activation(MROW[:, part * BW:(part + 1) * BW], ps[0:4, 4 + part, :], ACT.Copy)\
                                .then_inc(s("mrow"), 1)
                for q in range(4):
                    for t in range(2):
                        if p == after_turn(q, 2 + t):
                            input_context(2 * q + t)
                        if p == after_turn(q, 3 + t):
                            input_high(2 * q + t)

            for p in range(STARTED):
                if p not in WHOLE:
                    first_high(p)
                start(p)

            def evac_win(n):
                act.wait_ge(used, WIN0 + 8 * n + 8 + 4)
                sl = WIN_ORDER[n]
                if sl in (S_K, S_VAL, S_Q) and n < 2:
                    act.wait_ge(s("h_lo"), 8)
                if sl == S_K:
                    i = act.activation(KTT, ps[:, 0:4, :], ACT.Copy)
                elif sl == S_VAL:
                    i = act.activation(VAL, ps[:, 4:8, :], ACT.Copy)
                elif sl == S_Q:
                    i = act.activation(flat(ATT[:, 4096:5120]), pair(0), ACT.Copy, scale=float(P) ** -0.5)
                elif sl == S_LRU:
                    for g in range(G4):
                        i = act.activation(LP[:, g, :, 2:2 + T], ps[:, 4 + g, :].rearrange("p (s t) -> p s t", s=2), ACT.Copy)
                elif sl == S_POOL:
                    for b in range(2):
                        i = act.activation(ZP[:, 2 * b:2 * b + 2, PAD:PAD + T],
                                           ps[:, b, :].rearrange("p (g t) -> p g t", g=2), ACT.Copy)
                elif sl == S_V:
                    i = act.activation(V, pair(2), ACT.Copy)
                elif sl == S_U:
                    i = act.activation(flat(BR[:, 3104:4128]), pair(0), ACT.Copy)
                else:
                    act.wait_ge(s("pooled"), 1)
                    i = act.activation(flat(LG), pair(2), ACT.Copy)
                i.then_inc(s("win_read"), 1)

            def gate(f, n, b):
                act.wait_ge(used, f * BLK + (MIX0 + 8 * n + 8 + 4))
                if not isinstance(f, int):
                    act.wait_ge(s("merge_add"), f * 4 + (n + 1 - 4))
                elif n == 0:
                    act.wait_ge(s("att_out"), 4)
                elif n == 3:
                    act.wait_ge(s("gelu_made"), 1)
                act.activation(flat(S4[:, n, :]), pair(b), ACT.Sigmoid).then_inc(s("gate_read"), 1)

            def straight(w):
                if w % 8 == 3 and 8 < w < 68:
                    evac_win(w // 8 - 1)
                if w == 18:
                    act.wait_ge(s("params"), 1)
                    own.did(act.activation(LRC[:, 0, :], PB[:, PB_LAM:PB_LAM + 8], ACT.Abs))
                    own.wait()
                    act.activation(LRC[:, 1, :], LRC[:, 0, :], ACT.Exp, scale=-1.0).then_inc(s("explam"), 1)
                if w == 22:
                    act.wait_ge(s("wsp_turned"), 1)
                    act.activation(flat(BR[:, 11360:11872])[:, :, :], ps[:, 2, :].rearrange("p (b e) -> p b e", b=2), ACT.Copy)\
                        .then_inc(s("wspt"), 1)
                if w == 55:
                    act.wait_ge(s("v_stats"), 1)
                    act.activation(ST[:, 32:34], ST[:, 28:32].rearrange("p (t e) -> p t e", e=2)[:, :, 1], ACT.Sqrt,
                                   bias=EPSC[:, 0:1]).then_inc(s("v_std"), 1)
                for half, w0 in enumerate((ATT_A, ATT_B)):
                    if w == w0 + 4:
                        for u in range(4):
                            act.wait_ge(s("row_max"), 4 * half + u + 1)
                            act.activation(PR[:, u, :], ps[:, 4 + u, :], ACT.Exp, bias=ST[:, 8 + u:9 + u],
                                           accum_out=ST[:, 12 + u:13 + u]).then_inc(s("exps"), 1)
                    if w == w0 + 11:
                        for u in range(4):
                            act.wait_ge(s("p_turned"), 4 * half + u + 1)
                            if half:
                                act.wait_ge(s("att_av"), 2)
                            act.activation(PT[:, u // 2, :, u % 2 * P:u % 2 * P + P],
                                           ps[:, 4 + u, :].rearrange("p (j t) -> p j t", j=4), ACT.Copy).then_inc(s("pt"), 1)
                    if w == w0 + 16:
                        for hh in range(2):
                            act.wait_ge(s("att_av"), 2 * half + hh + 1)
                            act.wait_ge(s("h_last_read"), 1)
                            act.activation(Y[:, 12 + 2 * half + hh, 0, :], ps[:, 4 + 2 * hh, 0:T], ACT.Copy).then_inc(s("att_hi"), 1)
                if w == SMALL_MM + 4:
                    act.wait_ge(s("pool_mm"), 1)
                    for g in range(G4):
                        act.activation(Y[:, g, 0, :], ps[:, 4 + g // 2, g % 2 * T:g % 2 * T + T], ACT.Copy,
                                       scale=PB[:, PB_PS + g:PB_PS + g + 1]).then_inc(s("pool_hi"), 1)
                if w == SMALL_MM + 5:
                    act.wait_ge(s("sgu_float"), 1)
                    act.activation(Y[:, 4:8, 0, :], YF, ACT.Copy).then_inc(s("sgu_hi"), 1)
                if w == 70:
                    act.wait_ge(s("gelu_arg"), 1)
                    act.activation(S4[:, 3, :], S4[:, 3, :], ACT.Sigmoid, scale=2.0 * (2.0 / np.pi) ** 0.5).then_inc(s("gelu_sig"), 1)
                for g in range(G4):
                    if w == LRU_AT[g] + 4:
                        for d in range(2):
                            n = 2 * g + d
                            act.wait_ge(s("lru_mm"), n + 1)
                            if g:
                                act.wait_ge(s("lru_scan"), 2 * g - 1 + d)
                            else:
                                act.wait_ge(s("att_out"), 4)
                            col = d * 4 + g
                            act.activation(LT[:, d, 0, :], ps[:, 4 + 2 * d, :], ACT.Sigmoid, bias=PB[:, PB_BR + col:PB_BR + col + 1]).then_inc(s("lru_r"), 1)
                            act.activation(LT[:, d, 1, :], ps[:, 5 + 2 * d, :], ACT.Sigmoid, bias=PB[:, PB_BI + col:PB_BI + col + 1]).then_inc(s("lru_i"), 1)
                    if w == LRU_AT[g] + 5:
                        for d in range(2):
                            n = 2 * g + d
                            col = d * 4 + g
                            act.wait_ge(s("lru_r"), n + 1)
                            act.activation(LT[:, d, 2, :], LT[:, d, 0, :], ACT.Tanh, scale=LRC[:, 6, col:col + 1]).then_inc(s("lru_t"), 1)
                            act.activation(LT[:, d, 3, :], LT[:, d, 0, :], ACT.Exp, scale=LRC[:, 7, col:col + 1]).then_inc(s("lru_e"), 1)
                    if w == LRU_AT[g] + 7:
                        for d in range(2):
                            act.wait_ge(s("lru_w"), 2 * g + d + 1)
                            act.activation(LT[:, d, 2, :], LT[:, d, 2, :], ACT.Sqrt).then_inc(s("lru_s"), 1)
                    if w == LRU_AT[g] + 9:
                        act.wait_ge(s("lru_float"), g + 1)
                        act.activation(Y[:, 8 + g, 0, :], HS, ACT.Copy).then_inc(s("lru_hi"), 1)
                if w in (75, 83, 91, 99):
                    gate(0, (w - 75) // 8, 2 * ((w - 75) // 8 % 2))

            for w in range(8, 104):
                high((WIN0 + w) // 4, w % 4)
                straight(w)

            with act.Fori(1, 4) as f:
                for w in range(BLK):
                    high(f * (BLK // 4) + (MIX0 + w) // 4, w % 4)
                    if w in (11, 19, 27, 35):
                        n = (w - 11) // 8
                        gate(f, n, 2 * (n % 2))

            def merged_high(f):
                act.wait_ge(s("merge_add"), 4 * f + 4)
                act.wait_ge(used, MIX0 + 3 * BLK + 32 + 4)
                act.activation(HX[:, 4 * f:4 * f + 4, 0, :], MG[:, f, :].rearrange("p (k t) -> p k t", k=4), ACT.Copy)\
                    .then_inc(s("mg_hi"), 1)

            def x_columns(b):
                act.wait_ge(s("x_turned_again"), b + 1)
                act.activation(XM[:, b % 4 * 4:b % 4 * 4 + 4, b // 4 * P:b // 4 * P + P],
                               ps[:, 4 + b % 4, :].rearrange("p (k t) -> p k t", k=4), ACT.Copy).then_inc(s("xm_set"), 1)

            def square(n):
                act.wait_ge(s("xm_new"), n + 1)
                if n:
                    act.wait_ge(s("sq_used"), n)
                act.activation(SQ, XM[:, 4 * n:4 * n + 4, :], ACT.Square).then_inc(s("sq"), 1)

            merged_high(0)
            for n in range(4):
                for j in range(8):
                    w = 8 * n + j
                    high((OUT0 + 8 * n) // 4, j)
                    if w < 3:
                        merged_high(w + 1)
                    if 2 <= w < 10:
                        x_columns(w - 2)
                    if n and j == 5:
                        square(n - 1)
            high(FFN0 // 4, 0)
            high(FFN0 // 4, 1)
            square(3)
            act.activation(ST[:, 62:63], EPSC[:, 0:1], ACT.Sqrt)
            act.wait_ge(s("sq_used"), 4)
            act.activation(RSTD[:, :], ps[:, 6, 0:T], ACT.Sqrt, bias=EPSC[:, 0:1], scale=1.0 / D).then_inc(s("rms2"), 1)
            for q in range(8):
                b = MG[:, q // 2, q % 2 * 512:q % 2 * 512 + 512]
                act.wait_ge(s("h2_scaled"), q + 1)
                for t in range(2):
                    k = 2 * q + t
                    i = act.activation(b[:, t * T:t * T + T], b[:, t * T:t * T + T], ACT.Identity, bias=MC2[:, KT + k:KT + k + 1])
                i.then_inc(s("h2_float"), 1)
                act.wait_ge(s("h2_float"), q + 1)
                act.activation(HX[:, 2 * q:2 * q + 2, 0, :], flat(b), ACT.Copy).then_inc(s("h2_hi"), 1)
                high(FFN0 // 4, q + 2)

            def ffn_gate(m, last):
                act.wait_ge(used, last + 1 + 4)
                if isinstance(m, int) and m == 0:
                    act.wait_ge(s("h2_lo"), 8)
                else:
                    act.wait_ge(s("ffn_gate_read"), m)
                act.activation(flat(SG), pair(0), ACT.Sigmoid).then_inc(s("ffn_sig"), 1)

            def hidden_high(m, hid=HID):
                act.wait_ge(s("hid_float"), m + 1)
                act.activation(hid[:, :, 0, :], HD.rearrange("p (k t) -> p k t", k=4), ACT.Copy).then_inc(s("hid_hi"), 1)

            for w in range(10, 16):
                high(FFN0 // 4, w)
                if w == 11:
                    ffn_gate(0, FFN0 + 7)
            with act.Fori(1, FC - 1) as m:
                base = LOOP0 - 24 + m * 24
                for w in range(24):
                    high((LOOP0 - 24) // 4 + m * 6, w)
                    if w == 4:
                        hidden_high(m - 1)
                    if w == 11:
                        ffn_gate(m, base + 7)
            for w in range(32):
                high(PRE0 // 4, w)
                if w == 4:
                    hidden_high(FC - 2)
                if w == 11:
                    ffn_gate(FC - 1, PRE0 + 7)
                if w == 20:
                    hidden_high(FC - 1, HIDL)

            for i in range(8):
                act.wait_ge(s("y_turned"), i + 1)
                if i >= 2:
                    act.wait_ge(s("sqf"), i - 1)
                act.activation(SQ[:, i % 2 * BW:(i % 2 + 1) * BW], ps[:, i % 4, :], ACT.Square,
                               accum_out=ST[:, i % 2 * 4 + i // 2:i % 2 * 4 + i // 2 + 1]).then_inc(s("sqf"), 1)
            act.activation(ST[:, 63:64], EPSC[:, 0:1], ACT.Sqrt)
            act.wait_ge(s("sum_f"), 1)
            act.activation(ST[:, 10:12], ST[:, 8:10], ACT.Sqrt, bias=EPSC[:, 0:1], scale=1.0 / D).then_inc(s("rms3"), 1)
            act.wait_ge(s("rstd3"), 1)
            for half in range(2):
                cols = slice(half * D // 2, (half + 1) * D // 2)
                act.activation(OTOK[:, 0, cols], OTOK[:, 0, cols], ACT.Copy, scale=ST[:, 10:11]).then_inc(s("rows_done0"), 1)

        @block.vector
        def _(dve):
            own = Own(dve, own_v)
            tt, ts, stt = dve.tensor_tensor, dve.tensor_scalar, dve.scalar_tensor_tensor

            def first_low(p):
                dve.wait_ge(hi_done, p + 1)
                tt(LO[:, p % RING, :], raw_first(p), HI[:, p % RING, :], ALU.subtract).then_inc(lo_done, 2 if p + 1 in WHOLE else 1)

            def low(p, j):
                dve.wait_ge(hi_done, p + 1)
                tt(LO[:, j % RING, :], RAW[:, j % RING, :], HI[:, j % RING, :], ALU.subtract).then_inc(lo_done, 1)

            dve.memset(EPSC[:, :], EPS).then_inc(lo_done, 1)
            dve.memset(ST[:, 57:58], 0.0).then_inc(lo_done, 1)
            dve.memset(ST[:, 55:56], 0.0).then_inc(s("mod_used"), 1)
            dve.memset(ST[:, 56:57], 0.0).then_inc(s("mod_used"), 1)
            dve.memset(ST[:, 48:49], 0.0).then_inc(lo_done, 1)
            dve.memset(ST[:, 49:50], 0.0).then_inc(lo_done, 1)
            dve.memset(RP, 0.0).then_inc(s("rp_zero"), 1)
            dve.wait_ge(lo_done, 4)
            dve.memset(ST[:, 50:51], 0.0).then_inc(s("consts_set"), 1)
            dve.wait_ge(s("sigc"), 1)
            tt(SCF[:, :, :], ps[:, 6, 0:2 * KT].rearrange("p (w k) -> p w k", w=2),
               ST[:, 16:48].rearrange("p (w k) -> p w k", w=2), ALU.mult).then_inc(s("siluc"), 1)
            dve.wait_ge(s("siluc"), 1)
            dve.wait_ge(s("sc_hi"), 1)
            tt(SC[:, :, 2:4], SCF[:, :, :].rearrange("p w k -> p k w"), SC[:, :, 0:2], ALU.subtract).then_inc(s("sc_lo"), 1)

            def mod1_columns(q):
                dve.wait_ge(s("mod1_turned"), q + 1)
                rows = ps[:, 7, 0:32].rearrange("p (g k w) -> p g k w", g=2, w=4)
                mc = MC1.rearrange("p (g k) w -> p g k w", g=2)[:, :, 4 * q:4 * q + 4, :]
                bias = PA[:, PA_BMOD:PA_BMOD + 32].rearrange("p (g k) -> p g k", g=2)[:, :, 4 * q:4 * q + 4]
                own.did(tt(mc, rows[:, :, :, 0:2], bias.unsqueeze(3).to_broadcast([P, 2, 4, 2]), ALU.add)); own.wait()
                own.did(tt(mc, rows[:, :, :, 2:4], mc, ALU.add)); own.wait()
                stt(A1[:, 4 * q:4 * q + 4, :], MC1[:, KT + 4 * q:KT + 4 * q + 4, :], 1.0,
                    PA[:, PA_GMIX + 4 * q:PA_GMIX + 4 * q + 4].unsqueeze(2).to_broadcast([P, 4, 2]), ALU.add, ALU.mult)\
                    .then_inc(s("mod1_ready"), 1)
                dve.wait_ge(s("mod1_ready"), q + 1)

            def input_float(q):
                if q == 0:
                    dve.wait_ge(s("xt_act"), 8)
                    dve.wait_ge(s("xt_dve"), 8)
                for k in (2 * q, 2 * q + 1):
                    i = ts(XT[:, 1, k, :], XT[:, 1, k, :], A1[:, k, 0:1], MC1[:, k, 0:1], ALU.mult, ALU.add)
                i.then_inc(s("h_float"), 1)

            def input_low(q):
                dve.wait_ge(s("h_hi"), q + 1)
                tt(H[:, :, 2 * q:2 * q + 2, 1, :], XT[:, :, 2 * q:2 * q + 2, :], H[:, :, 2 * q:2 * q + 2, 0, :],
                   ALU.subtract).then_inc(s("h_lo"), 1)

            def start(p):
                if p == 13:
                    dve.wait_ge(s("params_turned"), 1)
                    own.did(dve.tensor_copy(PA[:, :], ps[:, 6, 0:P]))
                    own.did(dve.tensor_copy(PB[:, :], ps[:, 7, 0:PB_N]))
                    own.wait()
                    dve.memset(ST[:, 51:52], 0.0).then_inc(s("params"), 1)
                if p == 14:
                    dve.wait_ge(s("rms"), 1)
                    own.did(dve.reciprocal(ST[:, 4:8], ST[:, 4:8]))
                    own.wait()
                if 14 <= p < 18:
                    k = p - 14
                    ts(XTOK[:, k, :], XTOK[:, k, :], ST[:, 4 + k:5 + k], None, ALU.mult).then_inc(s("rows_scaled"), 1)
                if 20 <= p < 28:
                    b = 2 * (p - 20) + 1
                    dve.wait_ge(s("x_turned"), b + 1)
                    dve.tensor_copy(XT[:, b // 8, b % 4 * 4:b % 4 * 4 + 4, b // 4 % 2 * P:b // 4 % 2 * P + P],
                                    ps[:, b % 4, :].rearrange("p (k t) -> p k t", k=4)).then_inc(s("xt_dve"), 1)
                for q in range(4):
                    if p == after_turn(q, 1):
                        mod1_columns(q)
                    for t in range(2):
                        if p == after_turn(q, 2 + t):
                            input_float(2 * q + t)
                    for t in range(2):
                        if p == after_turn(q, 4 + t):
                            input_low(2 * q + t)

            for p in range(STARTED):
                if p not in WHOLE:
                    first_low(p)
                start(p)
            dve.memset(ST[:, 52:53], 0.0).then_inc(s("h_free"), 1)
            own.did(dve.memset(LP[:, :, :, 0:2], 0.0))
            own.did(dve.memset(LP[:, :, :, 2 + T:LW], 0.0))
            own.did(dve.memset(ZP[:, :, 0:PAD], 0.0))
            own.did(dve.memset(ZP[:, :, PAD + T:ZW], 0.0))

            def split_low(hi_sem, n, lo, src, hi_ap, done):
                dve.wait_ge(s(hi_sem), n)
                tt(lo, src, hi_ap, ALU.subtract).then_inc(s(done), 1)

            def mod_tile(g, k, acc):
                if isinstance(g, int) and g < EARLY:
                    src = MR[:, k % 2, :]
                    dve.wait_ge(s(f"mod_landed{k % 2}"), g * (KT // 2 * 16) + 16 * (k // 2 + 1))
                else:
                    src = MR4[:, k % 4, :]
                    dve.wait_ge(s(f"mod4_landed{k % 4}"), g * (KT // 4 * 16) + 16 * (k // 4 + 1 - EARLY * KT // 4))
                if k:
                    dve.wait_ge(s("mod_used"), g * KT + (k + 2))
                    i = stt(acc, src, SCF[:, 0, k:k + 1], acc, ALU.mult, ALU.add)
                else:
                    i = ts(acc, src, SCF[:, 0, k:k + 1], None, ALU.mult)
                i.then_inc(s("mod_used"), 1)

            def mod_columns(g, bank):
                dve.wait_ge(s("mod_turned"), g + 1)
                sums = MC2[:, bass.ds(g * 4, 4)]
                own.did(dve.reduce_sum(sums, ps[:, bank, :].rearrange("p (k n) -> p k n", k=4), AX_X))
                own.wait()
                tt(sums, sums, PA[:, bass.ds(g * 4 + 32, 4)], ALU.add).then_inc(s("mod_read"), 1)

            def straight(w):
                if MOD2_0 <= w < MOD2_0 + EARLY * KT:
                    mod_tile((w - MOD2_0) // 16, (w - MOD2_0) % 16, ACCM[:, (w - MOD2_0) // 16 % 2, :])
                if w in (47, 63):
                    mod_columns((w - 47) // 16, 0)
                if w == 20:
                    dve.wait_ge(s("explam"), 1)
                    own.did(ts(LRC[:, 2, :], LRC[:, 1, :], 2.0, None, ALU.add)); own.wait()
                    own.did(dve.reciprocal(LRC[:, 2, :], LRC[:, 2, :])); own.wait()
                    own.did(tt(LRC[:, 2, :], LRC[:, 2, :], LRC[:, 1, :], ALU.mult)); own.wait()
                    own.did(tt(LRC[:, 3, :], LRC[:, 2, :], LRC[:, 2, :], ALU.mult)); own.wait()
                    own.did(ts(LRC[:, 4, :], LRC[:, 3, :], 1.0 / 17, 1.0 / 15, ALU.mult, ALU.add)); own.wait()
                    for d in (13, 11, 9, 7, 5, 3, 1):
                        own.did(tt(LRC[:, 4, :], LRC[:, 4, :], LRC[:, 3, :], ALU.mult)); own.wait()
                        own.did(ts(LRC[:, 4, :], LRC[:, 4, :], 1.0 / d, None, ALU.add)); own.wait()
                    own.did(stt(LRC[:, 4, :], LRC[:, 4, :], 2.0, LRC[:, 2, :], ALU.mult, ALU.mult)); own.wait()
                    own.did(ts(LRC[:, 5, :], PB[:, PB_LAM:PB_LAM + 8], -1.0, 0.0, ALU.mult, ALU.max)); own.wait()
                    own.did(tt(LRC[:, 5, :], LRC[:, 5, :], LRC[:, 4, :], ALU.add)); own.wait()
                    own.did(ts(LRC[:, 6, :], LRC[:, 5, :], 4.0, None, ALU.mult))
                    own.did(ts(LRC[:, 7, :], LRC[:, 5, :], -8.0, None, ALU.mult))
                if w == 26:
                    dve.wait_ge(s("tb_in"), 16 * 8)
                    tt(TB.rearrange("p h j n -> p (h j) n"), TB.rearrange("p h j n -> p (h j) n"),
                       CST[:, CST_MASK:CST_MASK + GRID].unsqueeze(1).to_broadcast([P, 24, GRID]), ALU.add).then_inc(s("tb"), 1)
                for half, w0 in enumerate((ATT_A, ATT_B)):
                    if w == w0 + 4:
                        for u in range(4):
                            dve.wait_ge(s("scores"), 4 * half + u + 1)
                            dve.reduce_max(ST[:, 8 + u:9 + u], ps[:, 4 + u, :], AX_X, negate=True).then_inc(s("row_max"), 1)
                    if w == w0 + 6:
                        for u in range(4):
                            dve.wait_ge(s("exps"), 4 * half + u + 1)
                            own.did(dve.reciprocal(ST[:, 12 + u:13 + u], ST[:, 12 + u:13 + u]))
                        own.wait()
                        for u in range(4):
                            ts(PR[:, u, :], PR[:, u, :], ST[:, 12 + u:13 + u], None, ALU.mult).then_inc(s("probs"), 1)
                    if w == w0 + 17:
                        for hh in range(2):
                            split_low("att_hi", 2 * half + hh + 1, Y[:, 12 + 2 * half + hh, 1, :], ps[:, 4 + 2 * hh, 0:T],
                                      Y[:, 12 + 2 * half + hh, 0, :], "att_out")
                if w == 54:
                    dve.wait_ge(s("win_read"), 6)
                    for t in range(2):
                        own.did(dve.bn_stats(ST[:, 16 + 6 * t:22 + 6 * t], V[:, t, :]))
                    own.wait()
                    for t in range(2):
                        own.did(dve.bn_aggr(ST[:, 28 + 2 * t:30 + 2 * t], ST[:, 16 + 6 * t:22 + 6 * t]))
                    own.wait()
                    dve.memset(ST[:, 53:54], 0.0).then_inc(s("v_stats"), 1)
                if w == 56:
                    dve.wait_ge(s("v_std"), 1)
                    own.did(dve.reciprocal(ST[:, 32:34], ST[:, 32:34])); own.wait()
                    for t in range(2):
                        own.did(ts(V[:, t, :], V[:, t, :], ST[:, 28 + 2 * t:29 + 2 * t], ST[:, 32 + t:33 + t], ALU.subtract, ALU.mult))
                    own.wait()
                    dve.wait_ge(s("small_in"), 16 * 7)
                    for t in range(2):
                        tt(V[:, t, :], V[:, t, :], LNG, ALU.mult).then_inc(s("vn"), 1)
                if w in POOL_AT:
                    g, win = POOL_AT.index(w), POOL_WINDOWS[POOL_AT.index(w)]
                    if g == 0:
                        dve.wait_ge(s("win_read"), 5)
                        dve.wait_ge(s("small_in"), 16 * 7)
                        dve.wait_ge(s("p_turned"), 8)
                    cur, nxt = Z[:, 0, :], Z[:, 1, :]
                    own.did(tt(cur[:, 1:ZW], ZP[:, g, 0:ZW - 1], ZP[:, g, 1:ZW], ALU.add)); own.wait()
                    a, b, step = 1, ZW, 1
                    while 2 * step < win:
                        own.did(tt(nxt[:, a + step:b - step], cur[:, a:b - 2 * step], cur[:, a + 2 * step:b], ALU.add)); own.wait()
                        a, b, step, cur, nxt = a + step, b - step, 2 * step, nxt, cur
                    own.did(tt(YF[:, g, :], cur[:, PAD:PAD + T], RC[:, g, :], ALU.mult)); own.wait()
                    if g == G4 - 1:
                        tt(YF, YF, ZP[:, :, PAD:PAD + T], ALU.subtract).then_inc(s("pooled"), 1)
                if w == 69:
                    dve.wait_ge(s("win_read"), 8)
                    dve.wait_ge(s("att_av"), 4)
                    g3 = S4[:, 3, :]
                    own.did(tt(g3, LG, LG, ALU.mult)); own.wait()
                    own.did(ts(g3, g3, 0.044715, 1.0, ALU.mult, ALU.add)); own.wait()
                    tt(g3, g3, LG, ALU.mult).then_inc(s("gelu_arg"), 1)
                if w == 72:
                    dve.wait_ge(s("gelu_sig"), 1)
                    tt(LG, LG, S4[:, 3, :], ALU.mult).then_inc(s("gelu_made"), 1)
                    dve.wait_ge(s("gelu_made"), 1)
                if w == SMALL_MM + 5:
                    dve.wait_ge(s("pool_mm"), 1)
                    for g in range(G4):
                        if g == 0:
                            dve.wait_ge(s("pool_hi"), 4)
                        stt(Y[:, g, 1, :], ps[:, 4 + g // 2, g % 2 * T:g % 2 * T + T], PB[:, PB_PS + g:PB_PS + g + 1],
                            Y[:, g, 0, :], ALU.mult, ALU.subtract).then_inc(s("pool_lo"), 1)
                if w == SMALL_MM + 4:
                    dve.wait_ge(s("pool_mm"), 1)
                    dve.wait_ge(s("sgu_mm"), 1)
                    for t in range(2):
                        own.did(tt(YF[:, :, t * P:t * P + P], ps[:, 6 + t, :].rearrange("p (g t) -> p g t", g=4),
                                   BSP.rearrange("p (g t) -> p g t", g=4), ALU.add))
                    own.wait()
                    tt(YF, YF, U, ALU.mult).then_inc(s("sgu_float"), 1)
                if w == SMALL_MM + 6:
                    split_low("sgu_hi", 1, Y[:, 4:8, 1, :], YF, Y[:, 4:8, 0, :], "sgu_lo")
                for g in range(G4):
                    if w == LRU_AT[g] + 6:
                        z = Z[:, g % 2, :]
                        for d in range(2):
                            n = 2 * g + d
                            R, I, TH, EA = (LT[:, d, k, :] for k in range(4))
                            dve.wait_ge(s("lru_i"), n + 1)
                            own.did(tt(I, I, z, ALU.mult))
                            dve.wait_ge(s("lru_e"), n + 1)
                            own.did(stt(TH, EA, 1.0, TH, ALU.add, ALU.mult)); own.wait()
                            stt(TH, EA, 1.0, TH, ALU.add, ALU.mult).then_inc(s("lru_w"), 1)
                    if w == LRU_AT[g] + 8:
                        for d in range(2):
                            n = 2 * g + d
                            R, I, TH, EA = (LT[:, d, k, :] for k in range(4))
                            dve.wait_ge(s("lru_s"), n + 1)
                            own.did(tt(I, TH, I, ALU.mult)); own.wait()
                            if d == 0:
                                dve.tensor_tensor_scan(R, EA, I, 0.0, ALU.mult, ALU.add).then_inc(s("lru_scan"), 1)
                            else:
                                own.did(dve.tensor_tensor_scan(R[:, 0:T][:, ::-1], EA[:, 0:T][:, ::-1], I[:, 0:T][:, ::-1],
                                                               0.0, ALU.mult, ALU.add))
                                own.wait()
                                dve.tensor_tensor_scan(R[:, T:2 * T][:, ::-1], EA[:, T:2 * T][:, ::-1], I[:, T:2 * T][:, ::-1],
                                                       R[:, 0:1], ALU.mult, ALU.add).then_inc(s("lru_scan"), 1)
                        dve.wait_ge(s("lru_scan"), 2 * g + 2)
                        if g:
                            dve.wait_ge(s("lru_lo"), g)
                        own.did(tt(HS, LT[:, 0, 0, T:2 * T], LT[:, 1, 0, T:2 * T], ALU.add)); own.wait()
                        tt(HS, HS, LG[:, g * T:g * T + T], ALU.mult).then_inc(s("lru_float"), 1)
                    if w == LRU_AT[g] + 10:
                        split_low("lru_hi", g + 1, Y[:, 8 + g, 1, :], HS, Y[:, 8 + g, 0, :], "lru_lo")
                if w + 3 in LRU_AT:
                    g = LRU_AT.index(w + 3)
                    z = Z[:, g % 2, :].rearrange("p (s t) -> p s t", s=2)
                    dve.wait_ge(s("win_read"), 4)
                    if g == 0:
                        dve.wait_ge(s("pooled"), 1)
                    if g >= 2:
                        dve.wait_ge(s("lru_w"), 2 * (g - 1))
                    own.did(ts(z, LP[:, g, :, 0:T], PB[:, PB_CW + g:PB_CW + g + 1], PB[:, PB_CB + g:PB_CB + g + 1], ALU.mult, ALU.add))
                    for k in range(1, CONV):
                        own.wait()
                        i = stt(z, LP[:, g, :, k:k + T], PB[:, PB_CW + 4 * k + g:PB_CW + 4 * k + g + 1], z, ALU.mult, ALU.add)
                        if k < CONV - 1:
                            own.did(i)
                        else:
                            i.then_inc(s("conv"), 1)

            def merge(f, n, b):
                dve.wait_ge(used, f * BLK + (MIX0 + 34 + 2 * n + 4))
                dve.wait_ge(s("gate_read"), f * 4 + (n + 1))
                m = flat(MG[:, f, :]) if isinstance(f, int) else MG[:, bass.ds(f, 1), :].rearrange("p o (b e) -> p (o b) e", b=2)
                if n == 0:
                    tt(m, pair(b), flat(S4[:, n, :]), ALU.mult).then_inc(s("merge_read"), 1)
                    dve.wait_ge(s("merge_read"), f * 4 + (n + 1))
                    dve.memset(ST[:, 54:55], 0.0).then_inc(s("merge_add"), 1)
                else:
                    tt(flat(S4[:, n, :]), pair(b), flat(S4[:, n, :]), ALU.mult).then_inc(s("merge_read"), 1)
                    dve.wait_ge(s("merge_read"), f * 4 + (n + 1))
                    dve.wait_ge(s("merge_add"), f * 4 + n)
                    tt(m, m, flat(S4[:, n, :]), ALU.add).then_inc(s("merge_add"), 1)

            for w in range(8, 104):
                low(WIN0 + w, w % 4)
                straight(w)
                if w in (101, 103):
                    merge(0, (w - 101) // 2, (w - 101) % 4)
            dve.wait_ge(s("lru_lo"), 4)
            own.did(dve.tensor_copy(ACCB[:, 2, :], ACCM[:, 0, :]))
            own.wait()
            dve.memset(ONES, 1.0).then_inc(s("branches_made"), 1)

            with dve.Fori(1, 4) as f:
                own.enter(f, 1, 3)
                for w in range(BLK):
                    low(f * BLK + (MIX0 + w), w % 4)
                    for t in MOD_AT[w]:
                        mod_tile(f * 3 + t // KT, t % KT, ACCB[:, t // KT, :])
                    if w in (6, 21, 34):
                        mod_columns(f * 3 + (6, 21, 34).index(w) - 1, 4)
                    if w == 1:
                        merge(f - 1, 2, 0)
                    if w == 3:
                        merge(f - 1, 3, 2)
                    if w == 37:
                        merge(f, 0, 0)
                    if w == 39:
                        merge(f, 1, 2)
                own.leave(1, 3)

            def merged_low(f):
                split_low("mg_hi", f + 1, HX[:, 4 * f:4 * f + 4, 1, :], MG[:, f, :].rearrange("p (k t) -> p k t", k=4),
                          HX[:, 4 * f:4 * f + 4, 0, :], "mg_lo")

            def a2():
                dve.wait_ge(s("mod_read"), 12)
                stt(A2[:, :], MC2[:, 2 * KT:3 * KT], 1.0, PA[:, PA_GFFN:PA_GFFN + KT], ALU.add, ALU.mult).then_inc(s("a2"), 1)

            def residual(n):
                if n == 0:
                    dve.wait_ge(s("mod_read"), 4)
                    dve.wait_ge(s("xm_set"), 8)
                dve.wait_ge(used, OUT0 + 8 * n + 8 + 4)
                for k in range(4):
                    o = pair(2 * (n % 2))[:, k // 2, k % 2 * T:k % 2 * T + T]
                    i = stt(XM[:, 4 * n + k, :], o, MC2[:, 4 * n + k:4 * n + k + 1], XM[:, 4 * n + k, :], ALU.mult, ALU.add)
                i.then_inc(s("xm_new"), 1)

            merge(3, 2, 0)
            merged_low(0)
            for n in range(4):
                for j in range(8):
                    low(OUT0 + 8 * n + j, j)
                    if n == 0 and j < 3:
                        if j == 0:
                            merge(3, 3, 2)
                        merged_low(j + 1)
                    if 8 * n + j == 17:
                        mod_columns(11, 4)
                    if n and j == 3:
                        residual(n - 1)
                    if n == 2 and j >= 4:
                        dve.memset(ACC[:, j - 4, :], 0.0).then_inc(s("down_read"), 1)
            a2()
            low(FFN0, 0)
            low(FFN0 + 1, 1)
            residual(3)
            dve.wait_ge(s("a2"), 1)
            dve.wait_ge(s("rms2"), 1)
            own.did(dve.reciprocal(RSTD[:, :], RSTD[:, :])); own.wait()
            dve.wait_ge(s("xm_new"), 4)
            dve.wait_ge(used, OUT0 + 32 + 4)

            def h2_low(q):
                split_low("h2_hi", q + 1, HX[:, 2 * q:2 * q + 2, 1, :], flat(MG[:, q // 2, q % 2 * 512:q % 2 * 512 + 512]),
                          HX[:, 2 * q:2 * q + 2, 0, :], "h2_lo")

            for q in range(8):
                for t in range(2):
                    k = 2 * q + t
                    i = stt(MG[:, q // 2, (q % 2 * 2 + t) * T:(q % 2 * 2 + t + 1) * T], XM[:, k, :], A2[:, k:k + 1], RSTD[:, :],
                            ALU.mult, ALU.mult)
                i.then_inc(s("h2_scaled"), 1)
                if q:
                    h2_low(q - 1)
                    low(FFN0 + q + 1, q + 1)
            h2_low(7)

            def ffn_gated(m):
                dve.wait_ge(s("ffn_sig"), m + 1)
                tt(flat(TG), pair(0), flat(SG), ALU.mult).then_inc(s("ffn_gate_read"), 1)

            def hidden(m, last):
                dve.wait_ge(used, last + 1 + 4)
                dve.wait_ge(s("ffn_gate_read"), m + 1)
                tt(flat(HD), pair(2), flat(TG), ALU.mult).then_inc(s("hid_float"), 1)

            def hidden_low(m, hid=HID):
                dve.wait_ge(s("hid_hi"), m + 1)
                tt(hid[:, :, 1, :], HD.rearrange("p (k t) -> p k t", k=4), hid[:, :, 0, :], ALU.subtract).then_inc(s("hid_lo"), 1)

            def down(m, n, last):
                dve.wait_ge(used, last + 1 + 4)
                dve.wait_ge(s("down_read"), m * 4 + (n + 1))
                tt(flat(ACC[:, n, :]), pair(4 + 2 * (n % 2)), flat(ACC[:, n, :]), ALU.add).then_inc(s("down_read"), 1)

            for w in range(9, 16):
                low(FFN0 + w, w)
                if w == 12:
                    ffn_gated(0)

            def chunk(m, mod):
                base = LOOP0 - 24 + m * 24
                for w in range(24):
                    low(base + w, w)
                    if mod and w >= 8:
                        mod_tile(m + 11, w - 8, ACCG[:, bass.ds(m - 1, 1), :].rearrange("p o n -> p (o n)"))
                    if w == 3:
                        hidden(m - 1, base - 1)
                    if w == 5:
                        hidden_low(m - 1)
                    if w == 12:
                        ffn_gated(m)
                    if w in (13, 15, 17, 19):
                        n = (w - 13) // 2
                        down(m - 1, n, base + 9 + 2 * n)

            with dve.Fori(1, 5) as m:
                chunk(m, True)
            with dve.Fori(5, FC - 1) as m:
                chunk(m, False)
            g2 = MC2[:, 3 * KT:4 * KT]

            def final_add(n):
                for k in range(4):
                    kk = 4 * n + k
                    i = own.did(stt(XM[:, kk, :], ACC[:, n, k * T:k * T + T], g2[:, kk:kk + 1], XM[:, kk, :], ALU.mult, ALU.add))

            def final_down(n):
                dve.wait_ge(used, LAST0 + 2 * n + 2 + 4)
                for k in range(4):
                    kk = 4 * n + k
                    i = stt(XM[:, kk, :], ps[:, 4 + 2 * (n % 2) + k // 2, k % 2 * T:k % 2 * T + T], g2[:, kk:kk + 1], XM[:, kk, :],
                            ALU.mult, ALU.add)
                i.then_inc(s("xf_new"), 1)

            def final_rows(n):
                for t in range(2):
                    i = 2 * n + t
                    dve.wait_ge(s("sqf"), i + 1)
                    tt(OTOK[:, t, n * BW:(n + 1) * BW], ps[:, i % 4, :], GFB[:, n * BW:(n + 1) * BW], ALU.mult).then_inc(s("y_read"), 1)

            for w in range(32):
                low(PRE0 + w, w)
                if w == 3:
                    hidden(FC - 2, PRE0 - 1)
                if w == 5:
                    hidden_low(FC - 2)
                if w == 12:
                    ffn_gated(FC - 1)
                if w == 19:
                    hidden(FC - 1, PRE0 + 15)
                if w == 21:
                    hidden_low(FC - 1, HIDL)
                if w in (22, 23, 25, 27):
                    n = (22, 23, 25, 27).index(w)
                    down(FC - 2, n, PRE0 + 17 + 2 * n)
                if w == 26:
                    dve.wait_ge(s("gate2_turned"), 1)
                    own.did(dve.reduce_sum(g2, ps[:, 0:4, :].rearrange("p b (k n) -> p (b k) n", k=4), AX_X))
                    own.wait()
                    own.did(tt(g2, g2, PA[:, 80:96], ALU.add))
                    own.wait()
                    dve.wait_ge(s("down_read"), 4 * FC - 2)
                    final_add(0)
                if w == 28:
                    dve.wait_ge(s("down_read"), 4 * FC)
                    final_add(1)
                if w == 29:
                    final_add(2)
                    own.wait()
                    final_down(0)
                if w == 30:
                    final_add(3)
                    own.wait()
                if w == 31:
                    final_down(1)
            dve.wait_ge(s("gfb_in"), 16)
            final_rows(0)
            final_down(2)
            final_rows(1)
            final_down(3)
            final_rows(2)
            final_rows(3)
            own.did(dve.reduce_sum(ST[:, 8:10], ST[:, 0:8].rearrange("p (t n) -> p t n", t=2), AX_X))
            own.wait()
            dve.memset(ST[:, 58:59], 0.0).then_inc(s("sum_f"), 1)
            dve.wait_ge(s("rms3"), 1)
            dve.reciprocal(ST[:, 10:12], ST[:, 10:12]).then_inc(s("rstd3"), 1)
            dve.wait_ge(s("rstd3"), 1)
            dve.wait_ge(s("y_read"), 8)
            for half in range(2):
                cols = slice(half * D // 2, (half + 1) * D // 2)
                ts(OTOK[:, 1, cols], OTOK[:, 1, cols], ST[:, 11:12], None, ALU.mult).then_inc(s("rows_done1"), 1)

        @block.tensor
        def _(pe):
            mm = pe.matmul

            def turn(o, src, start=True):
                n = src.shape[0]
                return mm(o, src, IDENT[0:n, 0:n], start=start, stop=True, is_transpose=True, skip_group_check=True)

            def rows3(o, wh, wl, xh, xl, first, last):
                mm(o, wh, xh, start=first, stop=False, skip_group_check=True)
                mm(o, wh, xl, start=False, stop=False, skip_group_check=True)
                return mm(o, wl, xh, start=False, stop=last, skip_group_check=True)

            def ready(p):
                pe.wait_ge(lo_done, p + 1 + 4)

            def weights(j, t, f):
                a = slice(t * BW + f * P, t * BW + f * P + P)
                return HI[:, j % RING, a], LO[:, j % RING, a]

            def piece(p, j, moving, outs, k0, first, last):
                ready(p)
                for t in range(2):
                    xh, xl = moving(k0 + t)
                    for f in range(4):
                        o, opens = outs(f)
                        i = rows3(o, *weights(j, t, f), xh, xl, first and t == 0 and opens, last and t == 1)
                i.then_inc(used, 1)

            def piece_rows(p, j, lhs, outs, k0, first, last):
                ready(p)
                for t in range(2):
                    wh, wl = HI[:, j % RING, t * BW:(t + 1) * BW], LO[:, j % RING, t * BW:(t + 1) * BW]
                    for q, o in enumerate(outs):
                        xh, xl = lhs(k0 + t, q)
                        mm(o, xh, wh, start=first and t == 0, stop=False, skip_group_check=True)
                        mm(o, xh, wl, start=False, stop=False, skip_group_check=True)
                        i = mm(o, xl, wh, start=False, stop=last and t == 1, skip_group_check=True)
                i.then_inc(used, 1)

            def halves(b):
                return lambda f: (ps[:, b + f // 2, f % 2 * T:f % 2 * T + T], f % 2 == 0)

            def banks(b):
                return lambda f: (ps[:, b + f, :], True)

            def both(k):
                return H[:, :, k, 0, :], H[:, :, k, 1, :]

            def only_x(k):
                return HX[:, k, 0, :], HX[:, k, 1, :]

            def turned_tokens(k, q):
                a = slice(q % 2 * P, q % 2 * P + P)
                return H[:, q // 2, k, 0, a], H[:, q // 2, k, 1, a]

            pe.wait_ge(s("cst_in"), 16)
            pe.wait_ge(s("crow_in"), 32)
            turn(ps[:, 6, 0:2 * KT], CROW).then_inc(s("c_turned"), 1)
            for b in range(4):
                turn(ps[:, b, 0:P], IDENT).then_inc(used, 1)

            def start(p):
                if p == 9:
                    pe.wait_ge(s("rows_in"), 16 * 9)
                    pe.wait_ge(s("siluc"), 1)
                    turn(ps[:, 6, 0:P], PAROW)
                    turn(ps[:, 7, 0:PB_N], PBROW).then_inc(s("params_turned"), 1)
                if 16 <= p < 24:
                    i = p - 16
                    for b in (2 * i, 2 * i + 1):
                        pe.wait_ge(s("rows_scaled"), b // 4 + 1)
                        if i >= 2:
                            pe.wait_ge(s("xt_dve" if b % 2 else "xt_act"), i - 1)
                        for k in range(4):
                            kk = b % 4 * 4 + k
                            m = turn(ps[:, b % 4, k * P:k * P + P], XTOK[:, b // 4, kk * P:kk * P + P], start=k == 0)
                        m.then_inc(s("x_turned"), 1)
                if p in MOD_TURN:
                    q = MOD_TURN.index(p)
                    pe.wait_ge(s("mrow"), 2 * q + 2)
                    if q == 0:
                        pe.wait_ge(s("params"), 1)
                    if q:
                        pe.wait_ge(s("h_float"), 2 * q - 1)
                    for k in range(8):
                        m = turn(ps[:, 7, 4 * k:4 * k + 4], MROW[:, k * P:(k + 1) * P], start=k == 0)
                    m.then_inc(s("mod1_turned"), 1)

            for p, (kind, q, j) in enumerate(START):
                if kind == "keys":
                    pe.wait_ge(s("h_lo"), 2 * q + j + 1)
                    piece(p, p, both, banks(0), 4 * q + 2 * j, q + j == 0, q + j == 4)
                    start(p)
                    continue
                if p == 0:
                    pe.wait_ge(s("sc_lo"), 1)
                if q and j % 8 == 0:
                    pe.wait_ge(s("mrow"), 2 * q - 1 + j // 8)
                if p in WHOLE:
                    pe.wait_ge(landed_first[p % START_RING], 16 * (p // START_RING + 1))
                    for t in range(2):
                        i = mm(ps[0:2, 4 + j // 8, :], SCF[:, :, 2 * (j % 8) + t], raw_first(p)[:, t * BW:(t + 1) * BW],
                               start=False, stop=False, skip_group_check=True)
                else:
                    ready(p)
                    for t in range(2):
                        for w, part in enumerate((HI, LO)):
                            i = mm(ps[0:4, 4 + j // 8, :], SC[:, 2 * (j % 8) + t, :], part[:, p % RING, t * BW:(t + 1) * BW],
                                   start=j % 8 + t + w == 0, stop=j % 8 + t + w == 9, skip_group_check=True)
                i.then_inc(used, 1)
                start(p)

            def mod_turn(g, acc, bank):
                pe.wait_ge(s("mod_used"), g * KT + (KT + 2))
                for k in range(4):
                    i = turn(ps[:, bank, k * P:(k + 1) * P], acc[:, k * P:(k + 1) * P], start=k == 0)
                i.then_inc(s("mod_turned"), 1)

            def straight(w):
                if w in (44, 60):
                    g = (w - 44) // 16
                    pe.wait_ge(s("win_read"), (5, 7)[g])
                    mod_turn(g, ACCM[:, g % 2, :], 0)
                if w in (47, 63):
                    pe.wait_ge(s("mod_read"), (w - 31) // 16)
                if w == 18:
                    pe.wait_ge(s("small_in"), 16 * 7)
                    for g in range(G4):
                        i = turn(ps[:, 2, g * P:g * P + P], SW[:, 4 + g, :], start=g == 0)
                    i.then_inc(s("wsp_turned"), 1)
                for half, w0 in enumerate((ATT_A, ATT_B)):
                    if w == w0:
                        pe.wait_ge(s("win_read"), 4)
                        pe.wait_ge(s("tb"), 1)
                        if half:
                            pe.wait_ge(s("att_out"), 2)
                            pe.wait_ge(s("pt"), 4)
                        for u in range(4):
                            h, t = 2 * half + u // 2, u % 2
                            o = ps[:, 4 + u, :]
                            mm(o, QT[:, h, t * P:t * P + P], KTT[:, h, :], start=True, stop=False, skip_group_check=True)
                            mm(o[:, T:2 * T], IDENT, TB[:, h, 2 - 2 * t:6 - 2 * t, :], start=False, stop=True,
                               skip_group_check=True).then_inc(s("scores"), 1)
                    if w == w0 + 7:
                        for u in range(4):
                            pe.wait_ge(s("probs"), 4 * half + u + 1)
                            for j in range(4):
                                i = turn(ps[:, 4 + u, j * P:j * P + P], PR[:, u, j * P:j * P + P], start=j == 0)
                            i.then_inc(s("p_turned"), 1)
                    if w == w0 + 12:
                        for hh in range(2):
                            h = 2 * half + hh
                            pe.wait_ge(s("pt"), 4 * half + 2 * hh + 2)
                            for j in range(4):
                                i = mm(ps[:, 4 + 2 * hh, 0:T], VAL[:, j, h * P:h * P + P], PT[:, hh, j, :], start=j == 0,
                                       stop=j == 3, skip_group_check=True)
                            i.then_inc(s("att_av"), 1)
                if w == SMALL_MM:
                    pe.wait_ge(s("att_out"), 4)
                    pe.wait_ge(s("pooled"), 1)
                    for g in range(G4):
                        i = mm(ps[:, 4 + g // 2, g % 2 * T:g % 2 * T + T], SW[:, g, :], YF[:, g, :], start=g % 2 == 0,
                               stop=True, skip_group_check=True)
                    i.then_inc(s("pool_mm"), 1)
                    pe.wait_ge(s("vn"), 2)
                    pe.wait_ge(s("wspt"), 1)
                    for t in range(2):
                        for g in range(G4):
                            i = mm(ps[:, 6 + t, g * P:g * P + P], V[:, t, g * P:g * P + P], WSPT[:, g, :], start=g == 0,
                                   stop=True, skip_group_check=True)
                    i.then_inc(s("sgu_mm"), 1)
                for g in range(G4):
                    if w == LRU_AT[g]:
                        pe.wait_ge(s("conv"), g + 1)
                        pe.wait_ge(s("pool_lo"), 4)
                        pe.wait_ge(s("sgu_float"), 1)
                        if g:
                            pe.wait_ge(s("lru_i"), 2 * g)
                        for d in range(2):
                            mm(ps[:, 4 + 2 * d, :], SW[:, 8 + 4 * d + g, :], Z[:, g % 2, :], start=True, stop=True)
                            mm(ps[:, 5 + 2 * d, :], SW[:, 16 + 4 * d + g, :], Z[:, g % 2, :], start=True, stop=True)\
                                .then_inc(s("lru_mm"), 1)

            win_wait = {2: 1, 3: 2, 4: 3, 5: 1, 6: 5, 7: 6}
            for n, sl in enumerate(WIN_ORDER):
                if n == 0:
                    continue
                if n == 1:
                    pe.wait_ge(s("mrow"), 8)
                if n in win_wait:
                    pe.wait_ge(s("win_read"), win_wait[n])
                if n == 5:
                    pe.wait_ge(s("wspt"), 1)
                for j in range(8):
                    p = WIN0 + 8 * n + j
                    k0, first, last = 2 * j, j == 0, j == 7
                    if sl == S_LRU:
                        piece(p, j, both, banks(4), k0, first, last)
                    elif sl == S_VAL:
                        piece_rows(p, j, turned_tokens, [ps[:, 4 + q, :] for q in range(4)], k0, first, last)
                    elif sl == S_V:
                        piece_rows(p, j, lambda k, q: turned_tokens(k, 2 + q), [ps[:, 2 + q, :] for q in range(2)], k0, first, last)
                    else:
                        piece(p, j, only_x, halves(2 if sl == S_LG else 0), k0, first, last)
                    straight(8 * n + j)
                    if sl == S_LRU and j == 7:
                        mm(ps[:, 3, 0:2], IDENT, CST[:, 0:2], start=True, stop=True, skip_group_check=True).then_inc(s("h_last_read"), 1)

            def gate_group(base, n):
                for j in range(8):
                    piece(base + 8 * n + j, j, only_x, halves(2 * (n % 2)), 2 * j, j == 0, j == 7)
                    yield 8 * n + j

            def branch_group(base, n):
                for j in range(2):
                    piece(base + 32 + 2 * n + j, 2 * n + j, lambda k: (Y[:, k, 0, :], Y[:, k, 1, :]), halves(2 * (n % 2)),
                          4 * n + 2 * j, j == 0, j == 1)

            for n in range(NB):
                if n < 2:
                    pe.wait_ge(s("win_read"), 7 + n)
                else:
                    pe.wait_ge(s("gate_read"), n - 1)
                for w in gate_group(MIX0, n):
                    straight(64 + w)
            y_ready = ("pool_lo", "sgu_lo", "lru_lo", "att_out")
            for n in range(NB):
                pe.wait_ge(s(y_ready[n]), 1 if n == 1 else 4)
                if n < 2:
                    pe.wait_ge(s("gate_read"), 3 + n)
                else:
                    pe.wait_ge(s("merge_read"), n - 1)
                branch_group(MIX0, n)

            pe.wait_ge(s("branches_made"), 1)
            with pe.Fori(1, 4) as f:
                base = MIX0 + f * BLK
                for n in range(NB):
                    if n < 2:
                        pe.wait_ge(s("merge_read"), f * 4 + (n - 1))
                    else:
                        pe.wait_ge(s("gate_read"), f * 4 + (n - 1))
                    for w in gate_group(base, n):
                        if w in (2, 17, 30):
                            i = (2, 17, 30).index(w) - 1
                            pe.wait_ge(s("mod_read"), f * 3 + i)
                            mod_turn(f * 3 + i, ACCB[:, i % 3, :], 4)
                for n in range(NB):
                    if n < 2:
                        pe.wait_ge(s("gate_read"), f * 4 + (3 + n))
                    else:
                        pe.wait_ge(s("merge_read"), f * 4 + (n - 1))
                    branch_group(base, n)

            def x_turn(b):
                if b == 0:
                    pe.wait_ge(s("x_again"), 32)
                    pe.wait_ge(s("mod_read"), 11)
                if b >= 4:
                    pe.wait_ge(s("xm_set"), b - 3)
                for k in range(4):
                    kk = b % 4 * 4 + k
                    i = turn(ps[:, 4 + b % 4, k * P:k * P + P], XT2[:, b // 4, kk * P:kk * P + P], start=k == 0)
                i.then_inc(s("x_turned_again"), 1)

            def sum_squares(n, name, count, first, last):
                pe.wait_ge(s(name), count)
                for k in range(4):
                    i = mm(ps[:, 6, 0:T], ONES[:, :], SQ[:, k * T:k * T + T], start=first and k == 0, stop=last and k == 3,
                           skip_group_check=True)
                i.then_inc(s("sq_used"), 1)

            for n in range(4):
                if n < 2:
                    pe.wait_ge(s("merge_read"), 15 + n)
                else:
                    pe.wait_ge(s("xm_new"), n - 1)
                for j in range(8):
                    if n == 0 and j % 2 == 0:
                        pe.wait_ge(s("mg_lo"), j // 2 + 1)
                    piece(OUT0 + 8 * n + j, j, only_x, halves(2 * (n % 2)), 2 * j, j == 0, j == 7)
                    if n == 0:
                        x_turn(j)
                    if 8 * n + j == 12:
                        pe.wait_ge(s("xm_set"), 8)
                        mod_turn(11, ACCB[:, 2, :], 4)
                    if n and j == 7:
                        sum_squares(n - 1, "sq", n, n == 1, False)
            sum_squares(3, "sq", 4, False, True)

            for w in range(16):
                if w < 8:
                    pe.wait_ge(s("h2_lo"), w + 1)
                if w == 0:
                    pe.wait_ge(s("xm_new"), 4)
                piece(FFN0 + w, w, only_x, halves(2 * (w // 8)), w % 8 * 2, w % 8 == 0, w % 8 == 7)

            def down_group(base, n, hid=HID):
                for j in range(2):
                    piece(base + 2 * n + j, 2 * n + j, lambda k: (hid[:, k, 0, :], hid[:, k, 1, :]), halves(4 + 2 * (n % 2)),
                          2 * j, j == 0, j == 1)

            def gate_pieces(m, base):
                pe.wait_ge(s("ffn_gate_read"), m)
                for j in range(8):
                    piece(base + j, j, only_x, halves(0), 2 * j, j == 0, j == 7)

            def up_pieces(m, base):
                pe.wait_ge(s("hid_float"), m)
                for j in range(8):
                    piece(base + j, j, only_x, halves(2), 2 * j, j == 0, j == 7)

            def gate2_turn():
                pe.wait_ge(s("mod_used"), 16 * KT + 2)
                pe.wait_ge(s("ffn_gate_read"), FC)
                pe.wait_ge(s("hid_float"), FC)
                for k in range(KT):
                    i = turn(ps[:, k // 4, k % 4 * P:k % 4 * P + P], ACCG[:, k // 4, k % 4 * P:k % 4 * P + P], start=k % 4 == 0)
                i.then_inc(s("gate2_turned"), 1)

            def down_pieces(m, base, behind_second=None):
                pe.wait_ge(s("hid_lo"), m)
                for n in range(4):
                    pe.wait_ge(s("down_read"), m * 4 + (n - 1))
                    down_group(base, n)
                    if n == 1 and behind_second:
                        behind_second()

            with pe.Fori(1, FC - 1) as m:
                base = LOOP0 - 24 + m * 24
                gate_pieces(m, base)
                down_pieces(m, base + 8)
                up_pieces(m, base + 16)
            gate_pieces(FC - 1, PRE0)
            up_pieces(FC - 1, PRE0 + 8)
            down_pieces(FC - 1, PRE0 + 16, gate2_turn)
            pe.wait_ge(s("hid_lo"), FC)

            def rows_turn(n):
                pe.wait_ge(s("xf_new"), n + 1)
                if n >= 2:
                    pe.wait_ge(s("y_read"), 2 * n - 2)
                for t in range(2):
                    for k in range(4):
                        i = turn(ps[:, (2 * n + t) % 4, k * P:k * P + P], XM[:, 4 * n + k, t * P:t * P + P], start=k == 0)
                    i.then_inc(s("y_turned"), 1)

            for n in range(4):
                if n < 2:
                    pe.wait_ge(s("down_read"), FC * 4 + (n - 1))
                else:
                    pe.wait_ge(s("xf_new"), n - 1)
                down_group(LAST0, n, HIDL)
                if n:
                    rows_turn(n - 1)
            rows_turn(3)


_INS = ['x', 'c', 'ctx', 'c_ctx', 'w_mod', 'b_mod', 'g_mix', 'g_ffn', 'g_final', 'w_in', 'w_pool', 'pool_scale',
        'gmlp_ln_g', 'w_sp', 'b_sp', 'conv_w', 'conv_b', 'w_rg', 'b_rg', 'w_ig', 'b_ig', 'lru_lam', 'rpb',
        'w_branch', 'w_gate', 'w_out', 'w_ffn_gate', 'w_ffn_up', 'w_ffn_down']


def shape_constants():
    cst = np.zeros((P, CST_N), np.float32)
    cst[:, 0:P] = np.eye(P)
    col = np.arange(GRID)
    start = np.clip(col - WIN_C // 2, 0, GRID - WIN_C)
    ok = (col[None, :] >= start[:, None]) & (col[None, :] < start[:, None] + WIN_C)
    cst[:, CST_MASK:CST_MASK + GRID] = np.tile(np.where(ok, 0.0, MASKED), (2, 1))
    t = np.arange(T)
    rc = [1.0 / (np.clip(t + w // 2, 0, T) - np.clip(t - w // 2, 0, T)) for w in POOL_WINDOWS]
    return cst, np.concatenate(rc).astype(np.float32)


def kernel(**inputs):
    import concourse.bacc as _bacc
    from concourse.bass_utils import run_bass_kernel_spmd as _run

    nc = _bacc.Bacc("TRN2", target_bir_lowering=False, num_devices=1)
    arrays, args = {}, []
    cst, rc = shape_constants()
    for name, a in [(n, inputs[n]) for n in _INS] + [("cst", cst), ("rc", rc)]:
        a = np.ascontiguousarray(a)
        arrays[f"in_{name}"] = a
        args.append(nc.dram_tensor(f"in_{name}", a.shape, mybir.dt.from_np(a.dtype), kind="ExternalInput").ap())
    args.append(nc.dram_tensor("out_0", (1, T, D), F32, kind="ExternalOutput").ap())
    build(nc, *args)
    r = _run(nc, [arrays], core_ids=[0])
    return r.results[0]["out_0"]
```
